# Optimizing a Trainium2 kernel written in Bass

```python
import math
import jax, jax.numpy as jnp
from jax import lax
import numpy as np

D_MODEL = 1024
BATCH = 1
SEQ = 512
DEPTH = 1

D_G = D_MODEL // 4
N_GROUPS = 5
D_MIX = N_GROUPS * D_G
N_SUB = 4
HEAD_DIM = D_G // N_SUB
CONV_A = 3
CONV_D = 31
CHUNK = 128
POOL_WINDOWS = (2, 4, 8, 16)
MEM_LEN = 256
LN_EPS = 1e-5
DEEPNORM_ALPHA = (2.0 * DEPTH) ** 0.25
DEEPNORM_BETA = (8.0 * DEPTH) ** -0.25

SPLIT_SIZES = (D_G, D_G, D_G, D_G, D_G, D_G, D_G, D_G, D_G, D_MIX)
D_IN = sum(SPLIT_SIZES)
SPLIT_OFFSETS = tuple(int(o) for o in np.cumsum(SPLIT_SIZES)[:-1])


def layer_norm(x, g, b):
    xf = x.astype(jnp.float32)
    mu = jnp.mean(xf, axis=-1, keepdims=True)
    var = jnp.mean(jnp.square(xf - mu), axis=-1, keepdims=True)
    y = (xf - mu) * lax.rsqrt(var + LN_EPS) * g.astype(jnp.float32) + b.astype(jnp.float32)
    return y.astype(x.dtype)

def causal_depthwise_conv(x, w):
    k, c = w.shape
    return lax.conv_general_dilated(
        x, w[:, None, :].astype(x.dtype), window_strides=(1,), padding=[(k - 1, 0)],
        dimension_numbers=("NWC", "WIO", "NWC"), feature_group_count=c)

def short_gated_conv(xa, ba, ca, w_conv):
    return ba * causal_depthwise_conv(ca * xa, w_conv)

def spatial_gating(u, v, ln_g, ln_b, w_s, b_s):
    bn, s, _ = v.shape
    u = jax.nn.gelu(u)
    v = layer_norm(jax.nn.gelu(v), ln_g, ln_b)
    v = v.reshape(bn, s // CHUNK, CHUNK, N_SUB, HEAD_DIM)
    mask = jnp.tril(jnp.ones((CHUNK, CHUNK), dtype=bool))
    w = jnp.where(mask[None], w_s, jnp.zeros_like(w_s))
    mixed = jnp.einsum("hts,bcshd->bcthd", w, v) + b_s.T[:, :, None]
    return u * mixed.reshape(bn, s, D_G)

def multiscale_pool(xc, w_grp, scale):
    bn, s, _ = xc.shape
    xf = xc.astype(jnp.float32).reshape(bn, s, N_SUB, HEAD_DIM)
    cs = jnp.pad(jnp.cumsum(xf, axis=1), ((0, 0), (1, 0), (0, 0), (0, 0)))
    t = jnp.arange(s)
    win = jnp.array(POOL_WINDOWS, dtype=jnp.int32)
    lo = jnp.maximum(t[:, None] + 1 - win[None, :], 0)
    window_sum = cs[:, 1:] - cs[:, lo, jnp.arange(N_SUB)[None, :]]
    count = jnp.minimum(t[:, None] + 1, win[None, :]).astype(jnp.float32)
    y = (window_sum / count[None, :, :, None] - xf).astype(xc.dtype)
    y = jnp.einsum("bsgc,gcd->bsgd", y, w_grp)
    return y.reshape(bn, s, D_G) * scale

def conformer_conv(a, g, w_dw, b_dw, ln_g, ln_b, w_pw):
    h = a * jax.nn.sigmoid(g)
    h = causal_depthwise_conv(h, w_dw) + b_dw
    h = jax.nn.silu(layer_norm(h, ln_g, ln_b))
    return h @ w_pw

def memory_cross_attention(q, mem, w_kv):
    bn, s, _ = q.shape
    k, v = jnp.split(mem @ w_kv, 2, axis=-1)
    q = q.reshape(bn, s, N_SUB, HEAD_DIM)
    k = k.reshape(bn, -1, N_SUB, HEAD_DIM)
    v = v.reshape(bn, -1, N_SUB, HEAD_DIM)
    scores = jnp.einsum("bshd,bmhd->bhsm", q, k).astype(jnp.float32) * (1.0 / math.sqrt(HEAD_DIM))
    p = jax.nn.softmax(scores, axis=-1).astype(v.dtype)
    return jnp.einsum("bhsm,bmhd->bshd", p, v).reshape(bn, s, D_G)

def hybrid_mixer(x, mem, w_in, conv_a_w, sg_ln_g, sg_ln_b, sg_w, sg_b, pool_w, pool_scale,
                 cc_dw_w, cc_dw_b, cc_ln_g, cc_ln_b, cc_pw_w, w_kv, w_out):
    proj = x @ w_in
    xa, ba, ca, u, v, xc, da, dg, q, gate = jnp.split(proj, SPLIT_OFFSETS, axis=-1)
    y_a = short_gated_conv(xa, ba, ca, conv_a_w)
    y_b = spatial_gating(u, v, sg_ln_g, sg_ln_b, sg_w, sg_b)
    y_c = multiscale_pool(xc, pool_w, pool_scale)
    y_d = conformer_conv(da, dg, cc_dw_w, cc_dw_b, cc_ln_g, cc_ln_b, cc_pw_w)
    y_e = memory_cross_attention(q, mem, w_kv)
    h = jnp.concatenate([y_a, y_b, y_c, y_d, y_e], axis=-1) * jax.nn.silu(gate)
    return h @ w_out

def first_inputs(seed: int = 0) -> dict:
    key = jax.random.key(seed)
    ks = jax.random.split(key, 20)
    L = DEPTH

    def nrm(k, shape, scale):
        return jax.random.normal(k, shape, jnp.float32) * scale

    return {
        "x": nrm(ks[0], (BATCH, SEQ, D_MODEL), 1.0),
        "mem": nrm(ks[1], (BATCH, MEM_LEN, D_MODEL), 1.0),
        "w_in": nrm(ks[2], (L, D_MODEL, D_IN), D_MODEL ** -0.5),
        "conv_a_w": nrm(ks[3], (L, CONV_A, D_G), CONV_A ** -0.5),
        "sg_ln_g": 1.0 + nrm(ks[4], (L, D_G), 0.05),
        "sg_ln_b": nrm(ks[5], (L, D_G), 0.05),
        "sg_w": nrm(ks[6], (L, N_SUB, CHUNK, CHUNK), CHUNK ** -0.5),
        "sg_b": 1.0 + nrm(ks[7], (L, N_SUB, CHUNK), 0.1),
        "pool_w": nrm(ks[8], (L, N_SUB, HEAD_DIM, HEAD_DIM), HEAD_DIM ** -0.5),
        "pool_scale": 1.0 + nrm(ks[9], (L, D_G), 0.1),
        "cc_dw_w": nrm(ks[10], (L, CONV_D, D_G), CONV_D ** -0.5),
        "cc_dw_b": nrm(ks[11], (L, D_G), 0.02),
        "cc_ln_g": 1.0 + nrm(ks[12], (L, D_G), 0.05),
        "cc_ln_b": nrm(ks[13], (L, D_G), 0.05),
        "cc_pw_w": nrm(ks[14], (L, D_G, D_G), D_G ** -0.5),
        "w_kv": nrm(ks[15], (L, D_MODEL, 2 * D_G), D_MODEL ** -0.5),
        "w_out": nrm(ks[16], (L, D_MIX, D_MODEL), D_MIX ** -0.5 * DEEPNORM_BETA),
        "ln_g": 1.0 + nrm(ks[17], (L, D_MODEL), 0.05),
        "ln_b": nrm(ks[18], (L, D_MODEL), 0.05),
    }

def first_block(x, mem, w_in, conv_a_w, sg_ln_g, sg_ln_b, sg_w, sg_b, pool_w, pool_scale,
              cc_dw_w, cc_dw_b, cc_ln_g, cc_ln_b, cc_pw_w, w_kv, w_out, ln_g, ln_b):
    for l in range(DEPTH):
        y = hybrid_mixer(x, mem, w_in[l], conv_a_w[l], sg_ln_g[l], sg_ln_b[l], sg_w[l], sg_b[l],
                         pool_w[l], pool_scale[l], cc_dw_w[l], cc_dw_b[l], cc_ln_g[l], cc_ln_b[l],
                         cc_pw_w[l], w_kv[l], w_out[l])
        x = layer_norm(DEEPNORM_ALPHA * x + y, ln_g[l], ln_b[l])
    return x


DEPTH_2 = 2

N_MIXERS = 2
N_MLSTM = (DEPTH_2 + 1) // 2
N_HGRN = DEPTH_2 // 2
CHUNK_2 = 64
M_HEADS = 8
M_DV = D_MODEL // M_HEADS
M_DQK = M_DV // 2
M_QK = M_HEADS * M_DQK
M_V = M_HEADS * M_DV
M_PROJ = 2 * M_QK + 2 * M_V + 2 * M_HEADS
CONV_K = 4
IGATE_CAP = 15.0
HG_EXPAND = 128
HG_HEADS = D_MODEL // HG_EXPAND
HG_DK = HG_EXPAND
HG_DV = D_MODEL // HG_HEADS
HG_PROJ = 2 * HG_HEADS * HG_DK + 2 * D_MODEL
D_FF = 2816
N_EXPERTS = 8
TOP_K = 2
D_FF_EXPERT = D_FF // 2
EPS = 1e-6
NEG = -1e30
F_FLOOR = 1e-30


def rmsnorm(x, w):
    x32 = x.astype(jnp.float32)
    y = x32 * lax.rsqrt(jnp.mean(x32 * x32, axis=-1, keepdims=True) + EPS)
    return (y * w.astype(jnp.float32)).astype(x.dtype)

def head_rmsnorm(h, w):
    nh, dh = h.shape[1], h.shape[3]
    y = h * lax.rsqrt(jnp.mean(h * h, axis=-1, keepdims=True) + EPS)
    return y * w.astype(jnp.float32).reshape(1, nh, 1, dh)

def split_heads(a, nh):
    b, s, _ = a.shape
    return a.reshape(b, s, nh, -1).transpose(0, 2, 1, 3)

def merge_heads(a):
    b, h, s, d = a.shape
    return a.transpose(0, 2, 1, 3).reshape(b, s, h * d)

def to_chunks(a):
    b, h, s = a.shape[:3]
    return jnp.moveaxis(a.reshape((b, h, s // CHUNK_2, CHUNK_2) + a.shape[3:]), 2, 0)

def from_chunks(a):
    a = jnp.moveaxis(a, 0, 2)
    b, h, nc, l = a.shape[:4]
    return a.reshape((b, h, nc * l) + a.shape[4:])

def causal_conv(x, w, b):
    ch = x.shape[-1]
    y = lax.conv_general_dilated(x, w[:, None, :].astype(x.dtype), window_strides=(1,),
                                 padding=[(w.shape[0] - 1, 0)],
                                 dimension_numbers=('NWC', 'WIO', 'NWC'),
                                 feature_group_count=ch)
    return y + b.astype(x.dtype)

def mlstm_chunkwise(q, k, v, li, f_pre):
    bsz, nh, _, dk = q.shape
    dv = v.shape[-1]
    lf = jax.nn.log_sigmoid(f_pre)
    mask = jnp.tril(jnp.ones((CHUNK_2, CHUNK_2), dtype=bool))

    def step(carry, xs):
        c_st, n_st, m_st = carry
        qc, kc, vc, lic, lfc = xs
        b = jnp.cumsum(lfc, axis=-1)
        d = jnp.where(mask, b[..., :, None] - b[..., None, :] + lic[..., None, :], NEG)
        inter = b + m_st[..., None]
        m_t = jnp.maximum(inter, jnp.max(d, axis=-1))
        w_inter = jnp.exp(inter - m_t)
        s = jnp.einsum('bhtd,bhsd->bhts', qc, kc) * jnp.exp(d - m_t[..., None])
        num = (w_inter[..., None] * jnp.einsum('bhtd,bhdv->bhtv', qc, c_st)
               + jnp.einsum('bhts,bhsv->bhtv', s, vc))
        den = w_inter * jnp.einsum('bhtd,bhd->bht', qc, n_st) + jnp.sum(s, axis=-1)
        h = num / jnp.maximum(jnp.abs(den), jnp.exp(-m_t))[..., None]
        b_last = b[..., -1]
        dl = b_last[..., None] - b + lic
        m_new = jnp.maximum(b_last + m_st, jnp.max(dl, axis=-1))
        wk = jnp.exp(dl - m_new[..., None])
        decay = jnp.exp(b_last + m_st - m_new)
        c_new = decay[..., None, None] * c_st + jnp.einsum('bhs,bhsd,bhsv->bhdv', wk, kc, vc)
        n_new = decay[..., None] * n_st + jnp.einsum('bhs,bhsd->bhd', wk, kc)
        return (c_new, n_new, m_new), h

    init = (jnp.zeros((bsz, nh, dk, dv), jnp.float32),
            jnp.zeros((bsz, nh, dk), jnp.float32),
            jnp.zeros((bsz, nh), jnp.float32))
    _, hs = lax.scan(step, init, (to_chunks(q), to_chunks(k), to_chunks(v), to_chunks(li), to_chunks(lf)))
    return from_chunks(hs)

def hgrn2_chunkwise(q, k, log_f, v):
    bsz, nh, _, dk = q.shape
    dv = v.shape[-1]
    mask = jnp.tril(jnp.ones((CHUNK_2, CHUNK_2), dtype=bool))

    def step(s_st, xs):
        qc, kc, gc, vc = xs
        bc = jnp.cumsum(gc, axis=2)
        diff = bc[:, :, :, None, :] - bc[:, :, None, :, :]
        decay = jnp.exp(jnp.where(mask[:, :, None], diff, NEG))
        a = jnp.einsum('bhtd,bhsd,bhtsd->bhts', qc, kc, decay)
        o = (jnp.einsum('bhtd,bhdv->bhtv', qc * jnp.exp(bc), s_st)
             + jnp.einsum('bhts,bhsv->bhtv', a, vc))
        b_last = bc[:, :, -1]
        s_new = (jnp.exp(b_last)[..., None] * s_st
                 + jnp.einsum('bhsd,bhsv->bhdv', kc * jnp.exp(b_last[:, :, None] - bc), vc))
        return s_new, o

    init = jnp.zeros((bsz, nh, dk, dv), jnp.float32)
    _, os_ = lax.scan(step, init, (to_chunks(q), to_chunks(k), to_chunks(log_f), to_chunks(v)))
    return from_chunks(os_)

def mlstm_mixer(h, w_in, i_bias, f_bias, conv_w, conv_b, norm_w, w_out):
    proj = h @ w_in
    qk = jax.nn.silu(causal_conv(proj[..., :2 * M_QK], conv_w, conv_b))
    q = split_heads(qk[..., :M_QK], M_HEADS).astype(jnp.float32)
    k = split_heads(qk[..., M_QK:], M_HEADS).astype(jnp.float32) * (M_DQK ** -0.5)
    v = split_heads(proj[..., 2 * M_QK:2 * M_QK + M_V], M_HEADS).astype(jnp.float32)
    o = proj[..., 2 * M_QK + M_V:2 * M_QK + 2 * M_V]
    gates = proj[..., 2 * M_QK + 2 * M_V:].astype(jnp.float32)
    i_pre = gates[..., :M_HEADS] + i_bias.astype(jnp.float32)
    i_pre = IGATE_CAP * jnp.tanh(i_pre / IGATE_CAP)
    f_pre = gates[..., M_HEADS:] + f_bias.astype(jnp.float32)
    hh = mlstm_chunkwise(q, k, v, jnp.swapaxes(i_pre, 1, 2), jnp.swapaxes(f_pre, 1, 2))
    hh = merge_heads(head_rmsnorm(hh, norm_w)).astype(h.dtype) * jax.nn.sigmoid(o)
    return hh @ w_out

def hgrn2_mixer(h, w_in, lb, norm_w, w_out):
    proj = h @ w_in
    fd = HG_HEADS * HG_DK
    q = jax.nn.silu(proj[..., :fd]).astype(jnp.float32)
    f = proj[..., fd:2 * fd].astype(jnp.float32)
    i = proj[..., 2 * fd:2 * fd + D_MODEL].astype(jnp.float32)
    g = proj[..., 2 * fd + D_MODEL:]
    lb = lb.astype(jnp.float32)
    f_t = lb + (1.0 - lb) * jax.nn.sigmoid(f)
    log_f = jnp.log(jnp.maximum(f_t, F_FLOOR))
    k = (1.0 - lb) * jax.nn.sigmoid(-f)
    o = hgrn2_chunkwise(split_heads(q, HG_HEADS), split_heads(k, HG_HEADS),
                        split_heads(log_f, HG_HEADS), split_heads(i, HG_HEADS))
    o = merge_heads(head_rmsnorm(o, norm_w)).astype(h.dtype) * jax.nn.silu(g)
    return o @ w_out

def swiglu(t, wg, wu, wd):
    return (jax.nn.silu(t @ wg) * (t @ wu)) @ wd

def moe_swiglu(h, router_w, wg, wu, wd):
    bsz, s, d = h.shape
    t = h.reshape(bsz * s, d)
    logits = (t @ router_w).astype(jnp.float32)
    top_logits, top_idx = lax.top_k(logits, TOP_K)
    top_w = jax.nn.softmax(top_logits, axis=-1)
    gates = jnp.einsum('tk,tke->te', top_w, jax.nn.one_hot(top_idx, N_EXPERTS, dtype=jnp.float32)).astype(h.dtype)
    y = jnp.zeros_like(t)
    for e in range(N_EXPERTS):
        y = y + gates[:, e:e + 1] * swiglu(t, wg[e], wu[e], wd[e])
    return y.reshape(bsz, s, d)

def second_inputs(seed: int = 0) -> dict:
    key = jax.random.key(seed)
    ks = iter(jax.random.split(key, 32))

    def nrm(shape, scale):
        return jax.random.normal(next(ks), shape, jnp.float32) * scale

    d = D_MODEL
    return {
        'x': nrm((BATCH, SEQ, d), 1.0),
        'c': nrm((BATCH, d), 1.0),
        'ada_w': nrm((DEPTH_2, d, 6 * d), 0.5 * d ** -0.5),
        'ada_b': nrm((DEPTH_2, 6 * d), 0.02),
        'norm1_w': 1.0 + nrm((DEPTH_2, d), 0.02),
        'norm2_w': 1.0 + nrm((DEPTH_2, d), 0.02),
        'final_norm_w': 1.0 + nrm((d,), 0.02),
        'm_w_in': nrm((N_MLSTM, d, M_PROJ), d ** -0.5),
        'm_i_bias': nrm((N_MLSTM, M_HEADS), 0.1),
        'm_f_bias': jnp.linspace(3.0, 6.0, M_HEADS, dtype=jnp.float32)[None, :] + nrm((N_MLSTM, M_HEADS), 0.1),
        'm_conv_w': nrm((N_MLSTM, CONV_K, 2 * M_QK), CONV_K ** -0.5),
        'm_conv_b': nrm((N_MLSTM, 2 * M_QK), 0.01),
        'm_norm_w': 1.0 + nrm((N_MLSTM, M_V), 0.02),
        'm_w_out': nrm((N_MLSTM, M_V, d), M_V ** -0.5),
        'h_w_in': nrm((N_HGRN, d, HG_PROJ), d ** -0.5),
        'h_lb_logits': nrm((N_HGRN, HG_HEADS * HG_DK), 0.5),
        'h_norm_w': 1.0 + nrm((N_HGRN, d), 0.02),
        'h_w_out': nrm((N_HGRN, d, d), d ** -0.5),
        'ffn_w_gate': nrm((N_MLSTM, d, D_FF), d ** -0.5),
        'ffn_w_up': nrm((N_MLSTM, d, D_FF), d ** -0.5),
        'ffn_w_down': nrm((N_MLSTM, D_FF, d), D_FF ** -0.5),
        'moe_router': nrm((N_HGRN, d, N_EXPERTS), d ** -0.5),
        'moe_w_gate': nrm((N_HGRN, N_EXPERTS, d, D_FF_EXPERT), d ** -0.5),
        'moe_w_up': nrm((N_HGRN, N_EXPERTS, d, D_FF_EXPERT), d ** -0.5),
        'moe_w_down': nrm((N_HGRN, N_EXPERTS, D_FF_EXPERT, d), D_FF_EXPERT ** -0.5),
    }

def second_block(x, c, ada_w, ada_b, norm1_w, norm2_w, final_norm_w,
              m_w_in, m_i_bias, m_f_bias, m_conv_w, m_conv_b, m_norm_w, m_w_out,
              h_w_in, h_lb_logits, h_norm_w, h_w_out,
              ffn_w_gate, ffn_w_up, ffn_w_down,
              moe_router, moe_w_gate, moe_w_up, moe_w_down):
    cond = jax.nn.silu(c)
    gam = jax.nn.softmax(h_lb_logits.astype(jnp.float32), axis=0)
    lower_bounds = jnp.cumsum(gam, axis=0) - gam[:1]
    for layer in range(DEPTH_2):
        j = layer // N_MIXERS
        mod = (cond @ ada_w[layer] + ada_b[layer])[:, None, :]
        shift1, scale1, gate1, shift2, scale2, gate2 = jnp.split(mod, 6, axis=-1)
        hn = rmsnorm(x, norm1_w[layer]) * (1 + scale1) + shift1
        if layer % N_MIXERS == 0:
            y = mlstm_mixer(hn, m_w_in[j], m_i_bias[j], m_f_bias[j], m_conv_w[j], m_conv_b[j],
                            m_norm_w[j], m_w_out[j])
        else:
            y = hgrn2_mixer(hn, h_w_in[j], lower_bounds[j], h_norm_w[j], h_w_out[j])
        x = x + gate1 * y
        hn = rmsnorm(x, norm2_w[layer]) * (1 + scale2) + shift2
        if layer % 2 == 0:
            y = swiglu(hn, ffn_w_gate[j], ffn_w_up[j], ffn_w_down[j])
        else:
            y = moe_swiglu(hn, moe_router[j], moe_w_gate[j], moe_w_up[j], moe_w_down[j])
        x = x + gate2 * y
    return rmsnorm(x, final_norm_w)


def setup_inputs(seed=0):
    out = dict(first_inputs(seed))
    for name, value in second_inputs(seed + 1).items():
        if name != "x":
            out[name + "_2"] = value
    return out


def reference(
    x, mem, w_in, conv_a_w, sg_ln_g, sg_ln_b, sg_w, sg_b, pool_w, pool_scale, cc_dw_w, cc_dw_b,
    cc_ln_g, cc_ln_b, cc_pw_w, w_kv, w_out, ln_g, ln_b, c_2, ada_w_2, ada_b_2, norm1_w_2,
    norm2_w_2, final_norm_w_2, m_w_in_2, m_i_bias_2, m_f_bias_2, m_conv_w_2, m_conv_b_2,
    m_norm_w_2, m_w_out_2, h_w_in_2, h_lb_logits_2, h_norm_w_2, h_w_out_2, ffn_w_gate_2,
    ffn_w_up_2, ffn_w_down_2, moe_router_2, moe_w_gate_2, moe_w_up_2, moe_w_down_2,
):
    x = first_block(
        x, mem, w_in, conv_a_w, sg_ln_g, sg_ln_b, sg_w, sg_b, pool_w, pool_scale, cc_dw_w,
        cc_dw_b, cc_ln_g, cc_ln_b, cc_pw_w, w_kv, w_out, ln_g, ln_b,
    )
    return second_block(
        x, c_2, ada_w_2, ada_b_2, norm1_w_2, norm2_w_2, final_norm_w_2, m_w_in_2, m_i_bias_2,
        m_f_bias_2, m_conv_w_2, m_conv_b_2, m_norm_w_2, m_w_out_2, h_w_in_2, h_lb_logits_2,
        h_norm_w_2, h_w_out_2, ffn_w_gate_2, ffn_w_up_2, ffn_w_down_2, moe_router_2,
        moe_w_gate_2, moe_w_up_2, moe_w_down_2,
    )


_drawn_inputs = setup_inputs


def setup_inputs(seed=0):
    import zlib

    import numpy as np

    out = dict(_drawn_inputs(seed))
    spreads = {}
    factors = {'mem': 3.363,
     'sg_ln_g': 8.0,
     'sg_ln_b': 8.0,
     'sg_b': 4.582,
     'pool_scale': 3.612,
     'cc_dw_b': 8.0,
     'cc_ln_g': 6.406,
     'cc_ln_b': 6.761,
     'w_kv': 3.581,
     'norm1_w_2': 5.624,
     'norm2_w_2': 3.582,
     'final_norm_w_2': 8.894,
     'm_i_bias_2': 8.0,
     'm_conv_b_2': 55.938,
     'm_norm_w_2': 8.0,
     'h_norm_w_2': 8.0}
    for name, (base, spread) in spreads.items():
        noise = np.random.default_rng([zlib.crc32(name.encode()), seed]).standard_normal(out[name].shape)
        drawn = base * np.exp(spread * noise) if base else spread * noise
        out[name] = __import__('jax').numpy.asarray(drawn.astype(out[name].dtype))
    for name, factor in factors.items():
        out[name] = (out[name] * factor).astype(out[name].dtype)
    return out
```

```python
from contextlib import ExitStack

import concourse.bass as bass
from concourse import mybir

F32 = mybir.dt.float32
U32 = mybir.dt.uint32
ALU = mybir.AluOpType
ACT = mybir.ActivationFunctionType
AX = mybir.AxisListType.X

P = 128
S = 512
ST = S // P
D = 1024
KD = D // P
DG = 256
MEM = 256
TAPS_A, TAPS_D, TAPS_M = 3, 31, 4
HEADS = 8
FF = 2816
FFE = FF // 2
KF = FF // P
KE = FFE // P
EXPERTS = 8
ALPHA = 2.0 ** 0.25
SLOTS = 8
SLOT = 11 * P
BANKS = 4
BIG = 1e30

PARAMS = [("conv_a", TAPS_A * 2), ("sg_g", 2), ("sg_b", 2), ("pool_s", 2), ("dw_w", TAPS_D * 2), ("dw_b", 2),
          ("cc_g", 2), ("cc_b", 2), ("ln_g", 8), ("ln_b", 8), ("c", 8), ("ada_b", 96), ("norm1", 16),
          ("norm2", 16), ("final", 8), ("m_conv_w", TAPS_M * 8), ("m_conv_b", 8), ("m_norm", 8),
          ("lb", 8), ("h_norm", 8), ("mi_b", 1), ("mf_b", 1)]
CONSTS = [("ident", P), ("tri", P), ("neg", P), ("restart", S), ("pinv", 32), ("pwin", 2), ("eps5", 1),
          ("eps6", 1), ("iota", EXPERTS), ("one", 1)]
STREAM = [("kv", 4, KD), ("in", 28, KD), ("out", 8, 10), ("ada", 96, KD), ("m_in", 24, KD), ("m_out", 8, KD),
          ("ffn_up", 2 * KF, KD), ("ffn_down", 16, KE), ("h_in", 32, KD), ("h_out", 8, KD), ("moe", 30, KE)]


def columns(table):
    at, out = 0, {}
    for name, n in table:
        out[name] = (at, at + n)
        at += n
    return out, at


PCOL, NPAR = columns(PARAMS)
CCOL, NCST = columns(CONSTS)


class Link:

    def __init__(self, sem):
        self.sem, self.n = sem, 0

    def on(self, eng):
        def step(ins):
            self.n += 1
            ins.then_inc(self.sem, 1)
            eng.wait_ge(self.sem, self.n)
            return ins
        return step


class Stream:

    def __init__(self):
        self.uses, self.last, self.done = [0] * SLOTS, [0] * SLOTS, 0

    def place(self, n, kt, dram):
        plan = Plan()
        plan.n, plan.kt, plan.dram = n, kt, dram
        plan.done = self.done
        plan.uses = list(self.uses)
        plan.free = list(self.last)
        for b in range(n):
            self.uses[b % SLOTS] += 1
            self.last[b % SLOTS] = self.done + b + 1
        self.done += n
        return plan


class Plan:
    pass


def rows(i, n):
    return slice(i * n, (i + 1) * n)


class Chip:

    def __init__(self, nc, ctx):
        self.nc, self.ctx = nc, ctx
        sb = self.sb
        self.X = sb("x_res", [P, KD, S])
        self.HN = sb("x_norm", [P, KD, S])
        self.A = sb("act", [P, 32, S])
        self.W = sb("work", [P, 18, S])
        self.ring = sb("ring", [P, SLOTS, SLOT])
        self.par = sb("par", [P, NPAR])
        self.cst = sb("cst", [P, NCST])
        self.ones128 = sb("ones128", [P, P])
        self.ones256 = sb("ones256", [P, P])
        self.ones1024 = sb("ones1024", [P, P])
        self.ones = sb("ones", [P, P])
        self.lvl = sb("lvl", [P, 8, P], U32)
        self.sel = sb("sel", [HEADS, HEADS, P])
        self.sgw = sb("sgw", [P, 4, P])
        self.sgb = sb("sgb", [P, 2, P])
        self.plw = sb("plw", [P, 2, P])
        self.pw = sb("pw", [P, 2, DG])
        self.gw = sb("gw", [P, KD, 16])
        self.rw = sb("rw", [P, KD, EXPERTS])
        self.mod = sb("mod", [P, 96])
        self.cond = sb("cond", [P, KD])
        self.small = sb("small", [P, 64])
        self.ps = ctx.enter_context(nc.psum_tensor("banks", [P, 8, S], F32))
        self.loaded = [self.sem(f"slot{s}_loaded") for s in range(SLOTS)]
        self.blocks_done = self.sem("blocks_done")
        self.evac = self.sem("blocks_out")
        self.vlink, self.alink, self.glink, self.plink = (Link(self.sem(n)) for n in
                                                          ("dve_step", "act_step", "pool_step", "pe_step"))
        self.norm_in, self.norm_mean, self.norm_cent, self.norm_sq, self.norm_var, self.norm_std = (
            self.sem(n) for n in ("norm_in", "norm_mean", "norm_centred", "norm_squared", "norm_var", "norm_std"))
        self.norms = self.means = self.waited = 0
        self.stored = self.sem("stored")

    def sb(self, name, shape, dt=F32):
        return self.ctx.enter_context(self.nc.sbuf_tensor("sb_" + name, shape, dt))

    def sem(self, name):
        return self.ctx.enter_context(self.nc.semaphore(name))

    def p(self, name, i=None, n=1):
        a, b = PCOL[name]
        return self.par[:, a:b] if i is None else self.par[:, a + i:a + i + n]

    def c(self, name):
        a, b = CCOL[name]
        return self.cst[:, a:b]



def load_first(m, sp, plan):
    w = plan.kt * P
    for s in range(min(SLOTS, plan.n)):
        if plan.free[s]:
            sp.wait_ge(m.blocks_done, plan.free[s])
        sp.dma_start(m.ring[:, s, 0:w], plan.dram[s]).then_inc(m.loaded[s], 16)


def load_rest(m, sp, plan):
    w = plan.kt * P

    def load(b, s):
        sp.wait_ge(m.blocks_done, b + (plan.done + 1 - SLOTS))
        sp.dma_start(m.ring[:, s, 0:w], plan.dram[b]).then_inc(m.loaded[s], 16)

    turns = plan.n // SLOTS
    if turns > 1:
        with sp.Fori(1, turns) as i:
            for s in range(SLOTS):
                load(i * SLOTS + s, s)
    for b in range(max(turns, 1) * SLOTS, plan.n):
        load(b, b % SLOTS)


def product(m, pe, plan, block, loop=True):
    def one(b, s, use):
        pe.wait_ge(m.loaded[s], use * 16 + 16 * (plan.uses[s] + 1))
        out = b + (plan.done + 1 - BANKS)
        if not isinstance(out, int) or out > 0:
            pe.wait_ge(m.evac, out)
        block(m.ps[:, s % BANKS, :], m.ring[:, s, :]).then_inc(m.blocks_done, 1)

    turns = plan.n // SLOTS if loop else 0
    if turns:
        with pe.Fori(0, turns) as i:
            for s in range(SLOTS):
                one(i * SLOTS + s, s, i)
    for b in range(turns * SLOTS, plan.n):
        one(b, b % SLOTS, b // SLOTS)


def by_features(m, act, kt):
    def block(bank, w):
        for k in range(kt):
            last = m.nc.tensor.matmul(bank[:, 0:act.shape[2]], w[:, rows(k, P)], act[:, k, :],
                                      start=(k == 0), stop=(k == kt - 1))
        return last
    return block


def by_tokens(m, act, kt, tiles):
    def block(bank, w):
        for t in range(tiles):
            for k in range(kt):
                last = m.nc.tensor.matmul(bank[:, rows(t, P)], act[:, k, rows(t, P)], w[:, rows(k, P)],
                                          start=(k == 0), stop=(k == kt - 1))
        return last
    return block



class Norm:

    def __init__(self, m, v, ones, sq, std, eps, centred, waits=True, bank=4):
        m.norms += 1
        m.means += centred
        m.waited += waits
        self.k, self.mean_k, self.in_k = m.norms, centred and m.means, waits and m.waited
        self.v, self.ones, self.sq, self.std, self.eps, self.bank = v, ones, sq, std, eps, bank
        self.n = v.shape[1]

    def pe(self, m, pe):
        bank, nt = m.ps[:, self.bank, :], self.n
        if self.mean_k:
            if self.in_k:
                pe.wait_ge(m.norm_in, self.in_k)
            for i in range(nt):
                last = m.nc.tensor.matmul(bank, self.ones, self.v[:, i, :], start=(i == 0), stop=(i == nt - 1))
            last.then_inc(m.norm_mean, 1)
        pe.wait_ge(m.norm_sq, self.k)
        bank = m.ps[:, self.bank + 1, :]
        for i in range(nt):
            last = m.nc.tensor.matmul(bank, self.ones, self.sq[:, i, :], start=(i == 0), stop=(i == nt - 1))
        last.then_inc(m.norm_var, 1)

    def act(self, m, act):
        if self.mean_k:
            act.wait_ge(m.norm_cent, self.mean_k)
        elif self.in_k:
            act.wait_ge(m.norm_in, self.in_k)
        m.nc.scalar.activation(self.sq, self.v, ACT.Square).then_inc(m.norm_sq, 1)
        act.wait_ge(m.norm_var, self.k)
        m.nc.scalar.activation(self.std, m.ps[:, self.bank + 1, :], ACT.Sqrt, bias=self.eps).then_inc(m.norm_std, 1)

    def dve(self, m, dve):
        if self.mean_k:
            dve.wait_ge(m.norm_mean, self.mean_k)
            mean = m.ps[:, self.bank, :].unsqueeze(1).broadcast_to([P, self.n, S])
            m.nc.vector.tensor_tensor(self.v, self.v, mean, ALU.subtract).then_inc(m.norm_cent, 1)
        dve.wait_ge(m.norm_std, self.k)
        m.vlink.on(dve)(m.nc.vector.reciprocal(self.std, self.std))

    def spread(self, n=None):
        return self.std.unsqueeze(1).broadcast_to([P, n or self.n, S])


def give(eng, ins, sem, count):
    ins.then_inc(sem, 1)
    eng.wait_ge(sem, count)



DA, DGT, XC, XA, BA, CA, V, U, Q, GATE = 0, 2, 4, 6, 8, 10, 12, 14, 16, 18
YA, YB, YC, YD, YE = 0, 2, 4, 6, 8


def stage_setup(m, a):
    nc = m.nc
    m.s_small, m.s_x, m.s_mem, m.s_gel, m.s_const = (m.sem(n) for n in ("small_loaded", "x_loaded", "mem_loaded",
                                                                        "table_loaded", "consts_set"))
    m.memT = m.W[:, 14:18, :].rearrange("p a (b c) -> p (a b) c", c=MEM)
    with nc.Block() as block:
        @block.sync
        def _(sp):
            sp.dma_start(m.memT, a["memT"]).then_inc(m.s_mem, 16)
            load_first(m, sp, m.plans["kv"])
            sp.dma_start(m.X[:], a["xT"]).then_inc(m.s_x, 16)

        @block.scalar
        def _(act):
            for out, src in ((m.par[:], a["par"]), (m.cst[:], a["cst"]), (m.lvl[:], a["lvl"]), (m.sel[:], a["sel"]),
                             (m.sgw[:], a["sgw"]), (m.plw[0:64, 0, 0:64], a["plw"][0]),
                             (m.plw[64:128, 0, 64:128], a["plw"][1]), (m.plw[0:64, 1, 0:64], a["plw"][2]),
                             (m.plw[64:128, 1, 64:128], a["plw"][3]), (m.pw[:], a["pw"]), (m.gw[:], a["gw"]),
                             (m.rw[:], a["rw"])):
                act.dma_start(out, src).then_inc(m.s_small, 16)
            for h in range(4):
                act.dma_start(m.sgb[64 * (h % 2):64 * (h % 2) + 64, h // 2, :],
                              a["sgb"][h].partition_broadcast(64)).then_inc(m.s_small, 16)
            m.n_small = 16 * 16
            act.wait_ge(m.s_small, m.n_small)
            nc.scalar.activation(m.cond[:], m.p("c"), ACT.Silu).then_inc(m.alink.sem, 1)
            m.alink.n += 1
            act.wait_ge(m.alink.sem, m.alink.n)

        @block.vector
        def _(dve):
            step = m.vlink.on(dve)
            for t, v in ((m.ones128, 1 / P), (m.ones256, 1 / DG), (m.ones1024, 1 / D), (m.ones, 1.0)):
                step(nc.vector.memset(t[:], v))

        @block.gpsimd
        def _(pool):
            step = m.glink.on(pool)
            for lo, j in ((0, 64), (64, 0)):
                step(nc.gpsimd.memset(m.plw[lo:lo + 64, :, j:j + 64], 0.0))


def stage_project(m):
    nc, A, W = m.nc, m.A, m.W
    kv, inn, out = m.plans["kv"], m.plans["in"], m.plans["out"]
    m.kT, m.vm = A[:, 28, :].rearrange("p (j c) -> p j c", c=MEM), A[:, 29, :].rearrange("p (t c) -> p t c", c=DG)
    m.conv = W[:, 10:12, :]
    with nc.Block() as block:
        @block.sync
        def _(sp):
            load_first(m, sp, inn)
            load_rest(m, sp, inn)
            load_first(m, sp, out)

        @block.tensor
        def _(pe):
            pe.wait_ge(m.s_mem, 16)
            keys, values = by_features(m, m.memT, KD), by_tokens(m, m.memT, KD, 2)
            turn = iter((keys, keys, values, values))
            product(m, pe, kv, lambda bank, w: next(turn)(bank, w))
            pe.wait_ge(m.s_x, 16)
            product(m, pe, inn, by_features(m, m.X, KD))

        @block.scalar
        def _(act):
            step = m.alink.on(act)
            for b in range(4):
                act.wait_ge(m.blocks_done, kv.done + b + 1)
                if b < 2:
                    nc.scalar.activation(m.kT[:, b, :], m.ps[:, b, 0:MEM], ACT.Copy).then_inc(m.evac, 1)
                else:
                    nc.scalar.activation(m.vm[:, :, rows(b - 2, P)],
                                         m.ps[:, b, 0:2 * P].rearrange("p (t c) -> p t c", c=P),
                                         ACT.Copy).then_inc(m.evac, 1)
            for b in range(inn.n):
                act.wait_ge(m.blocks_done, inn.done + b + 1)
                how = (ACT.Sigmoid if DGT <= b < XC else ACT.Gelu_apprx_tanh if V <= b < Q else
                       ACT.Silu if b >= GATE else ACT.Copy)
                nc.scalar.activation(A[:, b, :], m.ps[:, b % BANKS, :], how).then_inc(m.evac, 1)

        @block.vector
        def _(dve):
            step = m.vlink.on(dve)
            ready = lambda tile: dve.wait_ge(m.evac, inn.done + tile)
            ready(XC)
            h = A[:, DA:DA + 2, :]
            step(nc.vector.tensor_tensor(h, h, A[:, DGT:DGT + 2, :], ALU.mult))
            for f in range(2):
                step(nc.vector.tensor_scalar(m.conv[:, f, :], h[:, f, :], m.p("dw_w", 2 * (TAPS_D - 1) + f),
                                             m.p("dw_b", f), ALU.mult, ALU.add))
            for back in range(1, TAPS_D):
                for f in range(2):
                    acc = m.conv[:, f, back:]
                    step(nc.vector.scalar_tensor_tensor(acc, h[:, f, :S - back],
                                                        m.p("dw_w", 2 * (TAPS_D - 1 - back) + f), acc,
                                                        ALU.mult, ALU.add))
            ready(XA)
            x, s, d = A[:, XC:XC + 2, :], W[:, 12:14, :], A[:, 30:32, :]

            def double(out, src, back):
                step(nc.vector.tensor_copy(out[:, :, :back], src[:, :, :back]))
                step(nc.vector.tensor_tensor(out[:, :, back:], src[:, :, back:], src[:, :, :S - back], ALU.add))

            double(s, x, 1)
            double(d, s, 2)
            step(nc.vector.tensor_copy(s[64:128, 0:1, :], d[64:128, 0:1, :]))
            double(s[:, 1:2, :], d[:, 1:2, :], 4)
            double(d[64:128, 1:2, :], s[64:128, 1:2, :], 8)
            step(nc.vector.tensor_copy(s[64:128, 1:2, :], d[64:128, 1:2, :]))
            for f in range(2):
                step(nc.vector.tensor_scalar(s[:, f, 16:], s[:, f, 16:], m.c("pwin")[:, f:f + 1], None, ALU.mult))
                step(nc.vector.tensor_tensor(s[:, f, 0:16], s[:, f, 0:16], m.c("pinv")[:, rows(f, 16)], ALU.mult))
            step(nc.vector.tensor_tensor(s, s, x, ALU.subtract))
            ready(V)
            z, y = A[:, CA:CA + 2, :], W[:, YA:YA + 2, :]
            step(nc.vector.tensor_tensor(z, z, A[:, XA:XA + 2, :], ALU.mult))
            for f in range(2):
                step(nc.vector.tensor_scalar(y[:, f, :], z[:, f, :], m.p("conv_a", 2 * 2 + f), None, ALU.mult))
                for back in (1, 2):
                    acc = y[:, f, back:]
                    step(nc.vector.scalar_tensor_tensor(acc, z[:, f, :S - back], m.p("conv_a", 2 * (2 - back) + f),
                                                        acc, ALU.mult, ALU.add))
            step(nc.vector.tensor_tensor(y, y, A[:, BA:BA + 2, :], ALU.mult))


def stage_mix(m):
    nc, A, W, ps = m.nc, m.A, m.W, m.ps
    v, u, vT = A[:, V:V + 2, :], A[:, U:U + 2, :], A[:, 30:32, :].rearrange("p a (b c) -> p (a b) c", c=DG)
    y = lambda j: W[:, j:j + 2, :]
    gated = lambda j: A[:, GATE + j:GATE + j + 2, :]
    sq, std, pooled = A[:, XC:XC + 2, :], A[:, XA, :], W[:, 12:14, :]
    prob = A[:, 2:4, :].rearrange("p a (b c) -> p (a b) c", c=MEM)
    prT = A[:, 0:2, :]
    norm_v = Norm(m, v, m.ones256[:], sq, std, m.c("eps5"), True, waits=False)
    norm_c = Norm(m, m.conv, m.ones256[:], sq, std, m.c("eps5"), True, waits=False)
    mx, nmx, rs, ri = (m.small[:, rows(i, 4)] for i in range(4))
    (vn_ready, vt_ready, vt_out, mixed, mixed_used, conv_ready, conv_act, pw_done, pool_done, score, score_top, probs,
     probs_scaled, pt_ready, pt_out, pv_done, masked, y_out) = (m.sem("mix_" + n) for n in (
         "v_normed", "v_turned", "v_turned_out", "gating", "gating_used", "conv_normed", "conv_silu", "pointwise",
         "pooled", "scores", "score_max", "exp", "probs", "probs_turned", "probs_turned_out", "attended", "masked",
         "attended_out"))
    with nc.Block() as block:
        @block.gpsimd
        def _(pool):
            for h in range(4):
                last = nc.gpsimd.tensor_tensor(m.sgw[:, h, :], m.sgw[:, h, :], m.c("tri"), ALU.mult)
                give(pool, last, masked, h + 1)

        @block.tensor
        def _(pe):
            norm_v.pe(m, pe)
            norm_c.pe(m, pe)
            pe.wait_ge(vn_ready, 1)
            for c in range(ST):
                for f in range(2):
                    last = nc.tensor.transpose(ps[:, 6 + c // 2, (c % 2) * DG + f * P:(c % 2) * DG + f * P + P],
                                               v[:, f, rows(c, P)], m.c("ident"))
            last.then_inc(vt_ready, 1)
            pe.wait_ge(vt_out, 1)
            pe.wait_ge(masked, 4)
            for h in range(4):
                lo = 64 * (h % 2)
                for c in range(ST):
                    last = nc.tensor.matmul(ps[lo:lo + 64, h // 2, rows(c, P)], vT[:, c, rows(h, 64)], m.sgw[:, h, :],
                                            start=True, stop=True)
            last.then_inc(mixed, 1)
            pe.wait_ge(conv_act, 1)
            for f in range(2):
                for k in range(2):
                    last = nc.tensor.matmul(ps[:, 2 + f, :], m.pw[:, k, rows(f, P)], m.conv[:, k, :],
                                            start=(k == 0), stop=(k == 1))
            last.then_inc(pw_done, 1)
            for f in range(2):
                last = nc.tensor.matmul(ps[:, 6 + f, :], m.plw[:, f, :], pooled[:, f, :], start=True, stop=True)
            last.then_inc(pool_done, 1)
            for h in range(4):
                lo = 64 * (h % 2)
                pe.wait_ge(mixed_used, 1 + 0 * h)
                if h:
                    pe.wait_ge(probs, h)
                for t in range(ST):
                    last = nc.tensor.matmul(ps[:, t // 2, rows(t % 2, MEM)], A[lo:lo + 64, Q + h // 2, rows(t, P)],
                                            m.kT[lo:lo + 64, h // 2, :], start=True, stop=True)
                last.then_inc(score, 1)
                pe.wait_ge(probs_scaled, h + 1)
                for k in range(2):
                    for t in range(ST):
                        last = nc.tensor.transpose(ps[:, 4 + k, rows(t, P)], prob[:, t, rows(k, P)], m.c("ident"))
                last.then_inc(pt_ready, 1)
                pe.wait_ge(pt_out, h + 1)
                if h == 0:
                    pe.wait_ge(y_out, 1)
                for k in range(2):
                    last = nc.tensor.matmul(ps[lo:lo + 64, 6 + h // 2, :], m.vm[:, k, rows(h, 64)], prT[:, k, :],
                                            start=(k == 0), stop=(k == 1))
                last.then_inc(pv_done, 1)

        @block.scalar
        def _(act):
            step = m.alink.on(act)
            norm_v.act(m, act)
            norm_c.act(m, act)
            act.wait_ge(vt_ready, 1)
            give(act, nc.scalar.activation(A[:, 30:32, :], ps[:, 6:8, :], ACT.Copy), vt_out, 1)
            act.wait_ge(conv_ready, 1)
            for f in range(2):
                last = nc.scalar.activation(m.conv[:, f, :], m.conv[:, f, :], ACT.Silu, bias=m.p("cc_b", f),
                                            scale=m.p("cc_g", f))
                if f == 0:
                    step(last)
            give(act, last, conv_act, 1)
            for h in range(4):
                act.wait_ge(score_top, h + 1)
                for t in range(ST):
                    last = nc.scalar.activation(prob[:, t, :], ps[:, t // 2, rows(t % 2, MEM)], ACT.Exp,
                                                bias=nmx[:, t:t + 1], scale=0.125, accum_out=rs[:, t:t + 1])
                    if t < ST - 1:
                        step(last)
                give(act, last, probs, h + 1)
                act.wait_ge(pt_ready, h + 1)
                give(act, nc.scalar.activation(prT, ps[:, 4:6, :], ACT.Copy), pt_out, h + 1)

        @block.vector
        def _(dve):
            step = m.vlink.on(dve)
            norm_v.dve(m, dve)
            step(nc.vector.tensor_tensor(v, v, norm_v.spread(), ALU.mult))
            step(nc.vector.tensor_scalar(v[:, 0, :], v[:, 0, :], m.p("sg_g", 0), m.p("sg_b", 0), ALU.mult, ALU.add))
            give(dve, nc.vector.tensor_scalar(v[:, 1, :], v[:, 1, :], m.p("sg_g", 1), m.p("sg_b", 1), ALU.mult,
                                              ALU.add), vn_ready, 1)
            norm_c.dve(m, dve)
            give(dve, nc.vector.tensor_tensor(m.conv, m.conv, norm_c.spread(), ALU.mult), conv_ready, 1)
            dve.wait_ge(mixed, 1)
            for f in range(2):
                step(nc.vector.tensor_tensor(W[:, YB + f, :].rearrange("p (c t) -> p c t", t=P),
                                             ps[:, f, :].rearrange("p (c t) -> p c t", t=P),
                                             m.sgb[:, f, :].unsqueeze(1).broadcast_to([P, ST, P]), ALU.add))
            step(nc.vector.tensor_tensor(y(YB), y(YB), u, ALU.mult))
            give(dve, nc.vector.tensor_tensor(y(YB), y(YB), gated(YB), ALU.mult), mixed_used, 1)
            step(nc.vector.tensor_tensor(y(YA), y(YA), gated(YA), ALU.mult))
            dve.wait_ge(pw_done, 1)
            step(nc.vector.tensor_tensor(y(YD), ps[:, 2:4, :], gated(YD), ALU.mult))
            dve.wait_ge(pool_done, 1)
            for f in range(2):
                last = nc.vector.scalar_tensor_tensor(W[:, YC + f, :], ps[:, 6 + f, :], m.p("pool_s", f),
                                                      A[:, GATE + YC + f, :], ALU.mult, ALU.mult)
                if f == 0:
                    step(last)
            give(dve, last, y_out, 1)
            for h in range(4):
                dve.wait_ge(score, h + 1)
                if h:
                    dve.wait_ge(probs, h)
                step(nc.vector.tensor_reduce(mx, ps[:, 0:2, :].rearrange("p a (b c) -> p (a b) c", c=MEM), AX,
                                             ALU.max))
                give(dve, nc.vector.tensor_scalar(nmx, mx, -0.125, None, ALU.mult), score_top, h + 1)
                dve.wait_ge(probs, h + 1)
                step(nc.vector.reciprocal(ri, rs))
                if h:
                    dve.wait_ge(pt_ready, h)
                give(dve, nc.vector.tensor_tensor(prob, prob, ri.unsqueeze(2).broadcast_to([P, ST, MEM]), ALU.mult),
                     probs_scaled, h + 1)
            dve.wait_ge(pv_done, 4)
            step(nc.vector.tensor_tensor(y(YE), ps[:, 6:8, :], gated(YE), ALU.mult))


def finish_norm_affine(m, dve, norm, scale, shift, out):
    nc, step = m.nc, m.vlink.on(dve)
    norm.dve(m, dve)
    for i in range(norm.n):
        step(nc.vector.scalar_tensor_tensor(out[:, i, :], norm.v[:, i, :], scale(i), norm.std, ALU.mult, ALU.mult))
        step(nc.vector.tensor_scalar(out[:, i, :], out[:, i, :], shift(i), None, ALU.add))


def stage_out(m):
    nc = m.nc
    plan, ada = m.plans["out"], m.plans["ada"]
    norm = Norm(m, m.X[:], m.ones1024[:], m.A[:, 0:8, :], m.A[:, 8, :], m.c("eps5"), True)
    with nc.Block() as block:
        @block.sync
        def _(sp):
            load_rest(m, sp, plan)
            load_first(m, sp, ada)

        @block.tensor
        def _(pe):
            product(m, pe, plan, by_features(m, m.W[:, 0:10, :], 10))
            norm.pe(m, pe)

        @block.vector
        def _(dve):
            for b in range(plan.n):
                dve.wait_ge(m.blocks_done, plan.done + b + 1)
                nc.vector.scalar_tensor_tensor(m.X[:, b, :], m.X[:, b, :], ALPHA, m.ps[:, b % BANKS, :], ALU.mult,
                                               ALU.add).then_inc(m.evac, 1)
            dve.wait_ge(m.evac, plan.done + plan.n)
            give(dve, nc.vector.memset(m.small[:, 0:1], 0.0), m.norm_in, norm.in_k)
            finish_norm_affine(m, dve, norm, lambda i: m.p("ln_g", i), lambda i: m.p("ln_b", i), m.X)

        @block.scalar
        def _(act):
            norm.act(m, act)


def stage_ada(m):
    nc, plan = m.nc, m.plans["ada"]
    with nc.Block() as block:
        @block.sync
        def _(sp):
            load_rest(m, sp, plan)
            load_first(m, sp, m.plans["m_in"])

        @block.tensor
        def _(pe):
            product(m, pe, plan, by_features(m, m.cond[:].unsqueeze(2), KD))

        @block.scalar
        def _(act):
            with act.Fori(0, plan.n // SLOTS) as i:
                for s in range(SLOTS):
                    act.wait_ge(m.blocks_done, i * SLOTS + (plan.done + s + 1))
                    nc.scalar.activation(m.mod[:, bass.ds(i * SLOTS + s, 1)], m.ps[:, s % BANKS, 0:1],
                                         ACT.Copy).then_inc(m.evac, 1)

        @block.vector
        def _(dve):
            step = m.vlink.on(dve)
            dve.wait_ge(m.evac, plan.done + plan.n)
            step(nc.vector.tensor_tensor(m.mod[:], m.mod[:], m.p("ada_b"), ALU.add))
            for layer in range(2):
                for half, w in ((0, "norm1"), (1, "norm2")):
                    at = layer * 48 + half * 24 + 8
                    step(nc.vector.tensor_scalar(m.mod[:, at:at + 8], m.mod[:, at:at + 8], 1.0, None, ALU.add))
                    step(nc.vector.tensor_tensor(m.mod[:, at:at + 8], m.mod[:, at:at + 8],
                                                 m.p(w, layer * 8, 8), ALU.mult))


def shift_of(m, layer, half):
    return lambda i: m.mod[:, layer * 48 + half * 24 + i:layer * 48 + half * 24 + i + 1]


def scale_of(m, layer, half):
    return lambda i: m.mod[:, layer * 48 + half * 24 + 8 + i:layer * 48 + half * 24 + 9 + i]


def gate_of(m, layer, half):
    return lambda i: m.mod[:, layer * 48 + half * 24 + 16 + i:layer * 48 + half * 24 + 17 + i]



def stage_modulate(m, layer, half):
    norm = Norm(m, m.X[:], m.ones1024[:], m.W[:, 0:8, :], m.W[:, 8, :], m.c("eps6"), False, waits=False)
    with m.nc.Block() as block:
        @block.tensor
        def _(pe):
            norm.pe(m, pe)

        @block.scalar
        def _(act):
            norm.act(m, act)

        @block.vector
        def _(dve):
            finish_norm_affine(m, dve, norm, scale_of(m, layer, half), shift_of(m, layer, half), m.HN)


def stage_m_project(m):
    nc, A, W, ps = m.nc, m.A, m.W, m.ps
    plan = m.plans["m_in"]
    m.g = {n: W[0:HEADS, 17 - j, :] for j, n in enumerate(("i", "f", "t", "m"))}
    g = m.g
    m.cT = W[:, 13, 0:ST * HEADS].rearrange("p (t h) -> p t h", h=HEADS)
    gates, gate_in, gate_soft, f_ready, em_in, conv_in, c_ready, cT_ready = (m.sem("m_" + n) for n in (
        "gates", "gate_rows", "gate_funcs", "forget", "floor_in", "conv_in", "decay", "decay_turned"))
    with nc.Block() as block:
        @block.sync
        def _(sp):
            load_rest(m, sp, plan)
            load_first(m, sp, m.plans["m_out"])

        @block.tensor
        def _(pe):
            for j in range(2):
                for k in range(KD):
                    last = nc.tensor.matmul(ps[0:HEADS, 4 + j, :], m.gw[:, k, rows(j, HEADS)], m.HN[:, k, :],
                                            start=(k == 0), stop=(k == KD - 1))
            last.then_inc(gates, 1)
            parts = by_features(m, m.HN, KD), by_tokens(m, m.HN, KD, ST)
            turn = iter([parts[0]] * 8 + [parts[1]] * 8 + [parts[0]] * 8)
            product(m, pe, plan, lambda bank, w: next(turn)(bank, w), loop=False)
            pe.wait_ge(c_ready, 1)
            for t in range(ST):
                last = nc.tensor.transpose(ps[:, 6, rows(t, HEADS)], g["i"][:, rows(t, P)],
                                           m.c("ident")[0:HEADS, 0:HEADS])
            last.then_inc(cT_ready, 1)

        @block.scalar
        def _(act):
            step = m.alink.on(act)
            act.wait_ge(gate_in, 1)
            step(nc.scalar.activation(g["i"], g["i"], ACT.Tanh, scale=1 / 15.0))
            step(nc.scalar.activation(g["t"], g["t"], ACT.Exp, scale=-1.0))
            give(act, nc.scalar.activation(g["t"], g["t"], ACT.Ln, bias=m.c("one")[0:HEADS, :]), gate_soft, 1)
            for b in range(plan.n):
                act.wait_ge(m.blocks_done, plan.done + b + 1)
                how = ACT.Sigmoid if b >= 16 else ACT.Copy
                nc.scalar.activation(A[:, b, :], ps[:, b % BANKS, :], how).then_inc(m.evac, 1)
                if b == 9:
                    act.wait_ge(conv_in, 1)
                if 9 <= b < 16:
                    act.wait_ge(conv_in, b - 8)
                    step(nc.scalar.activation(A[:, b - 9, :], A[:, b - 9, :], ACT.Silu, bias=m.p("m_conv_b", b - 9)))
            act.wait_ge(conv_in, 8)
            step(nc.scalar.activation(A[:, 7, :], A[:, 7, :], ACT.Silu, bias=m.p("m_conv_b", 7)))
            act.wait_ge(em_in, 1)
            step(nc.scalar.activation(g["f"], g["m"], ACT.Exp, scale=-1.0))

        @block.vector
        def _(dve):
            step = m.vlink.on(dve)
            dve.wait_ge(gates, 1)
            step(nc.vector.tensor_scalar(g["i"], ps[0:HEADS, 4, :], m.p("mi_b")[0:HEADS, :], None, ALU.add))
            step(nc.vector.tensor_scalar(g["f"], ps[0:HEADS, 5, :], m.p("mf_b")[0:HEADS, :], None, ALU.add))
            give(dve, nc.vector.scalar_tensor_tensor(g["t"], g["f"], -1.0, g["f"], ALU.mult, ALU.max), gate_in, 1)
            dve.wait_ge(gate_soft, 1)
            step(nc.vector.scalar_tensor_tensor(g["t"], g["f"], 0.0, g["t"], ALU.min, ALU.subtract))
            one = W[0:HEADS, 12, :]
            step(nc.vector.memset(one, 1.0))
            step(nc.vector.tensor_tensor_scan(out=g["m"], data0=one, data1=g["t"], initial=0.0, op0=ALU.mult,
                                              op1=ALU.add))
            give(dve, nc.vector.scalar_tensor_tensor(g["i"], g["i"], 15.0, g["m"], ALU.mult, ALU.subtract),
                 c_ready, 1)
            step(nc.vector.tensor_tensor_scan(out=g["t"], data0=one, data1=g["i"], initial=0.0, op0=ALU.mult,
                                              op1=ALU.max))
            give(dve, nc.vector.tensor_tensor(g["m"], g["m"], g["t"], ALU.add), em_in, 1)
            step(nc.vector.tensor_scalar(g["t"], g["t"], -1.0, None, ALU.mult))
            for b in range(8):
                dve.wait_ge(m.evac, plan.done + b + 1)
                x, y = W[:, b % 2, :], A[:, b, :]
                step(nc.vector.tensor_copy(x, y))
                step(nc.vector.tensor_scalar(y, x, m.p("m_conv_w", 8 * (TAPS_M - 1) + b), None, ALU.mult))
                for back in range(1, TAPS_M):
                    last = nc.vector.scalar_tensor_tensor(y[:, back:], x[:, :S - back],
                                                          m.p("m_conv_w", 8 * (TAPS_M - 1 - back) + b), y[:, back:],
                                                          ALU.mult, ALU.add)
                    if back < TAPS_M - 1:
                        step(last)
                give(dve, last, conv_in, b + 1)
            dve.wait_ge(cT_ready, 1)
            step(nc.vector.tensor_copy(m.cT, ps[:, 6, 0:ST * HEADS].rearrange("p (t h) -> p t h", h=HEADS)))


def stage_m_heads(m):
    nc, A, W, ps, g = m.nc, m.A, m.W, m.ps, m.g
    prob, den, sq = W[:, 0:4, :], W[:, 4, :], W[:, 5:6, :]
    dec = W[:, 6:10, :]
    spread, edge, decay, score, prob_ready, summed, h_out = (m.sem("mh_" + n) for n in (
        "rows", "edge", "decay", "scores", "weights", "summed", "head"))
    norms = [Norm(m, A[:, 8 + h:9 + h, :], m.ones128[:], sq, W[:, 10, :], m.c("eps6"), False, bank=4)
             for h in range(HEADS)]
    with nc.Block() as block:
        @block.tensor
        def _(pe):
            for h in range(HEADS):
                lo = 64 * (h % 2)
                if h:
                    pe.wait_ge(h_out, h)
                nc.tensor.matmul(ps[:, 4, :], m.sel[:, h, :], g["t"], start=True, stop=True)
                nc.tensor.matmul(ps[:, 7, :], m.sel[:, h, :], g["f"], start=True, stop=True).then_inc(spread, 1)
                for i in range(ST):
                    last = nc.tensor.matmul(ps[:, i, i * P:], A[lo:lo + 64, 4 + h // 2, rows(i, P)],
                                            A[lo:lo + 64, h // 2, i * P:], start=True, stop=True)
                last.then_inc(score, 1)
                pe.wait_ge(prob_ready, h + 1)
                for lhs, bank in ((None, 5), (m.ones[:], 6)):
                    for i in range(ST):
                        last = nc.tensor.matmul(ps[:, bank, i * P:], A[:, 8 + h, rows(i, P)] if lhs is None else lhs,
                                                prob[:, i, i * P:], start=(i == 0), stop=(i == ST - 1))
                last.then_inc(summed, 1)
                norms[h].pe(m, pe)

        @block.scalar
        def _(act):
            step = m.alink.on(act)
            for h in range(HEADS):
                act.wait_ge(edge, h + 1)
                for i in range(ST):
                    c = m.cT[:, i, h:h + 1]
                    last = nc.scalar.activation(dec[:, i, rows(i, P)], dec[:, i, rows(i, P)], ACT.Exp, bias=c)
                    if i < ST - 1:
                        step(last)
                        step(nc.scalar.activation(dec[:, i, (i + 1) * P:], ps[:, 4, (i + 1) * P:], ACT.Exp, bias=c))
                give(act, last, decay, h + 1)
                norms[h].act(m, act)

        @block.vector
        def _(dve):
            step = m.vlink.on(dve)
            for h in range(HEADS):
                dve.wait_ge(spread, h + 1)
                for i in range(ST):
                    last = nc.vector.tensor_tensor(dec[:, i, rows(i, P)], ps[:, 4, rows(i, P)], m.c("neg"), ALU.add)
                    if i < ST - 1:
                        step(last)
                give(dve, last, edge, h + 1)
                dve.wait_ge(decay, h + 1)
                dve.wait_ge(score, h + 1)
                for i in range(ST):
                    last = nc.vector.scalar_tensor_tensor(prob[:, i, i * P:], ps[:, i, i * P:], 0.125,
                                                          dec[:, i, i * P:], ALU.mult, ALU.mult)
                    if i < ST - 1:
                        step(last)
                give(dve, last, prob_ready, h + 1)
                dve.wait_ge(summed, h + 1)
                step(nc.vector.tensor_copy(den, ps[:, 7, :]))
                step(nc.vector.scalar_tensor_tensor(den, ps[:, 6, :], -1.0, den, ALU.mult, ALU.max))
                step(nc.vector.tensor_tensor(den, den, ps[:, 6, :], ALU.max))
                step(nc.vector.reciprocal(den, den))
                y = A[:, 8 + h, :]
                give(dve, nc.vector.tensor_tensor(y, ps[:, 5, :], den, ALU.mult), m.norm_in, norms[h].in_k)
                norms[h].dve(m, dve)
                step(nc.vector.scalar_tensor_tensor(y, y, m.p("m_norm", h), norms[h].std, ALU.mult, ALU.mult))
                give(dve, nc.vector.tensor_tensor(y, y, A[:, 16 + h, :], ALU.mult), h_out, h + 1)


def stage_residual(m, name, act_in, kt, gate, nxt, halves=1):
    nc, plan = m.nc, m.plans[name]
    with nc.Block() as block:
        @block.sync
        def _(sp):
            load_rest(m, sp, plan)
            if nxt:
                load_first(m, sp, m.plans[nxt])

        @block.tensor
        def _(pe):
            parts = [by_features(m, act_in[:, h * kt:(h + 1) * kt, :], kt) for h in range(halves)]
            turn = iter(parts * plan.n)
            product(m, pe, plan, lambda bank, w: next(turn)(bank, w))

        @block.vector
        def _(dve):
            step = m.vlink.on(dve)
            for b in range(plan.n):
                dve.wait_ge(m.blocks_done, plan.done + b + 1)
                x = m.X[:, b // halves, :]
                nc.vector.scalar_tensor_tensor(x, m.ps[:, b % BANKS, :], gate(b // halves), x, ALU.mult,
                                               ALU.add).then_inc(m.evac, 1)
                if halves > 1:
                    dve.wait_ge(m.evac, plan.done + b + 1)


def stage_ffn(m):
    nc, A, W, ps = m.nc, m.A, m.W, m.ps
    plan = m.plans["ffn_up"]
    silu, = (m.sem("ffn_silu"),)
    pairs = SLOTS // 2
    with nc.Block() as block:
        @block.sync
        def _(sp):
            load_rest(m, sp, plan)
            load_first(m, sp, m.plans["ffn_down"])

        @block.tensor
        def _(pe):
            product(m, pe, plan, by_features(m, m.HN, KD))

        turns, rest = divmod(plan.n // 2, pairs)

        @block.scalar
        def _(act):
            def one(j, s):
                act.wait_ge(m.blocks_done, j * 2 + (plan.done + 1))
                out = j * 2 + (plan.done - 2)
                act.wait_ge(m.evac, out)
                nc.scalar.activation(W[:, s % 2, :], ps[:, 2 * s % BANKS, :], ACT.Silu).then_inc(silu, 1)
            with act.Fori(0, turns) as i:
                for s in range(pairs):
                    one(i * pairs + s, s)
            for s in range(rest):
                one(turns * pairs + s, s)

        @block.vector
        def _(dve):
            def one(j, s):
                dve.wait_ge(silu, j + 1)
                dve.wait_ge(m.blocks_done, j * 2 + (plan.done + 2))
                out = A[:, bass.ds(j, 1), :] if not isinstance(j, int) else A[:, j:j + 1, :]
                nc.vector.tensor_tensor(out, W[:, s % 2:s % 2 + 1, :], ps[:, (2 * s + 1) % BANKS:(2 * s + 1) % BANKS + 1, :],
                                        ALU.mult).then_inc(m.evac, 2)
            with dve.Fori(0, turns) as i:
                for s in range(pairs):
                    one(i * pairs + s, s)
            for s in range(rest):
                one(turns * pairs + s, s)


LEVELS = 8
LN_EDGE = 2.0 ** -60
F_FLOOR = 1e-30
CROSS = [(0, 1), (2, 3), (1, 2), (1, 3), (0, 2), (0, 3)]


def stage_h_project(m):
    nc, A, W, ps = m.nc, m.A, m.W, m.ps
    plan = m.plans["h_in"]
    lb, oml, ex = m.small[:, 16:24], m.small[:, 24:32], m.small[:, 32:40]
    lb_in, lb_exp, both, log_in, log_out = (m.sem("h_" + n) for n in ("lb_in", "lb_exp", "sigmoids", "log_in", "logs"))
    with nc.Block() as block:
        @block.sync
        def _(sp):
            load_rest(m, sp, plan)
            load_first(m, sp, m.plans["h_out"])

        @block.tensor
        def _(pe):
            parts = by_features(m, m.HN, KD), by_tokens(m, m.HN, KD, ST)
            turn = iter([parts[0]] * 16 + [parts[1]] * 8 + [parts[0]] * 8)
            product(m, pe, plan, lambda bank, w: next(turn)(bank, w), loop=False)

        @block.scalar
        def _(act):
            step = m.alink.on(act)
            act.wait_ge(lb_in, 1)
            give(act, nc.scalar.activation(ex, ex, ACT.Exp), lb_exp, 1)
            for b in range(plan.n):
                act.wait_ge(m.blocks_done, plan.done + b + 1)
                bank = ps[:, b % BANKS, :]
                if 8 <= b < 16:
                    nc.scalar.activation(W[:, b - 8, :], bank, ACT.Sigmoid, scale=-1.0).then_inc(both, 1)
                    nc.scalar.activation(A[:, b, :], bank, ACT.Sigmoid).then_inc(m.evac, 1)
                else:
                    nc.scalar.activation(A[:, b, :], bank, ACT.Copy if 16 <= b < 24 else ACT.Silu).then_inc(m.evac, 1)
            for h in range(HEADS):
                act.wait_ge(log_in, h + 1)
                lo = W[:, 8 + h % 2, :]
                step(nc.scalar.activation(lo, lo, ACT.Ln, scale=1.0 / LN_EDGE))
                give(act, nc.scalar.activation(A[:, 8 + h, :], A[:, 8 + h, :], ACT.Ln), log_out, h + 1)

        @block.vector
        def _(dve):
            step = m.vlink.on(dve)
            give(dve, nc.vector.tensor_tensor(ex, m.p("lb"), m.p("lb"), ALU.subtract), lb_in, 1)
            dve.wait_ge(lb_exp, 1)
            step(nc.vector.reciprocal(oml, ex))
            step(nc.vector.tensor_tensor(ex, ex, oml, ALU.mult))
            step(nc.vector.tensor_tensor(lb, ex, ex, ALU.subtract))
            step(nc.vector.tensor_scalar(oml, lb, -1.0, 1.0, ALU.mult, ALU.add))

            def logs(h):
                dve.wait_ge(log_out, h + 1)
                f = A[:, 8 + h, :]
                step(nc.vector.tensor_tensor(f, f, W[:, 8 + h % 2, :], ALU.add))
                step(nc.vector.tensor_tensor_scan(out=W[:, 10, :], data0=m.c("restart"), data1=f, initial=0.0,
                                                  op0=ALU.mult, op1=ALU.add))
                step(nc.vector.tensor_copy(f, W[:, 10, :]))

            for h in range(HEADS):
                dve.wait_ge(m.evac, plan.done + 8 + h + 1)
                dve.wait_ge(both, h + 1)
                if h >= 2:
                    logs(h - 2)
                k, f, lo = W[:, h, :], A[:, 8 + h, :], W[:, 8 + h % 2, :]
                step(nc.vector.tensor_scalar(k, k, oml[:, h:h + 1], None, ALU.mult))
                step(nc.vector.tensor_scalar(f, f, oml[:, h:h + 1], lb[:, h:h + 1], ALU.mult, ALU.add))
                step(nc.vector.tensor_scalar(lo, f, F_FLOOR, LN_EDGE, ALU.max, ALU.min))
                give(dve, nc.vector.tensor_scalar(f, f, LN_EDGE, None, ALU.max), log_in, h + 1)
            for h in range(HEADS - 2, HEADS):
                logs(h)


def stage_h_heads(m):
    nc, A, W, ps, H = m.nc, m.A, m.W, m.ps, m.HN
    t_ready, e_ready, q_ready, k_ready, level_done, level_out, edge_in, cross_in, cross_done, cross_out, head_in, \
        head_done, h_out = (m.sem("hh_" + n) for n in (
            "diff", "decay", "q", "k", "level", "level_out", "edge_decay", "cross_in", "cross", "cross_out",
            "head_in", "head", "head_out"))
    tile4 = lambda t: t.rearrange("p (t c) -> p t c", c=P)
    att, cross = tile4(W[:, 11, :]), W[:, 12:14, :].rearrange("p a (t c) -> p (a t) c", c=P)
    eq, ek, q1, k1, k0 = W[:, 14, :], W[:, 15, :], W[:, 16, :], W[:, 17, :], W[:, 8, 0:P]
    norms = [Norm(m, A[:, h:h + 1, :], m.ones128[:], H[:, 6:7, :], H[:, 7, :], m.c("eps6"), False, bank=4)
             for h in range(HEADS)]
    with nc.Block() as block:
        @block.tensor
        def _(pe):
            for h in range(HEADS):
                q, k = A[:, h, :], W[:, h, :]
                for j in range(LEVELS):
                    n = h * LEVELS + j
                    if n >= 2:
                        pe.wait_ge(level_out, n - 1)
                    if j:
                        pe.wait_ge(q_ready, h * 7 + j)
                        pe.wait_ge(k_ready, h * 7 + j)
                    lhs, rhs = (H[:, 4 + j % 2, :], H[:, 2 + j % 2, :]) if j else (k, q)
                    for t in range(ST):
                        last = nc.tensor.matmul(ps[:, n % 2, rows(t, P)], lhs[:, rows(t, P)], rhs[:, rows(t, P)],
                                                start=True, stop=True)
                    last.then_inc(level_done, 1)
                pe.wait_ge(cross_in, h + 1)
                for i, (s, t) in enumerate(CROSS):
                    lhs = k0 if s == 0 and t > 1 else k1[:, rows(s, P)]
                    rhs = ek[:, rows(3, P)] if t == 3 and s < 2 else q1[:, rows(t, P)]
                    last = nc.tensor.matmul(ps[:, 2 + i // 4, rows(i % 4, P)], lhs, rhs, start=True, stop=True)
                last.then_inc(cross_done, 1)
                pe.wait_ge(level_out, (h + 1) * LEVELS)
                pe.wait_ge(cross_out, h + 1)
                for t in range(ST):
                    parts = [(t, att[:, t, :])] + [(s, cross[:, i, :]) for i, (s, tt) in enumerate(CROSS) if tt == t]
                    for i, (s, w) in enumerate(parts):
                        last = nc.tensor.matmul(ps[:, 6, rows(t, P)], A[:, 16 + h, rows(s, P)], w, start=(i == 0),
                                                stop=(i == len(parts) - 1))
                last.then_inc(head_done, 1)
                norms[h].pe(m, pe)

        @block.scalar
        def _(act):
            step = m.alink.on(act)
            for h in range(HEADS):
                b = A[:, 8 + h, :]
                if h:
                    act.wait_ge(cross_done, h)
                step(nc.scalar.activation(eq[:, P:], b[:, P:], ACT.Exp))
                for t in range(ST - 1):
                    last = nc.scalar.activation(ek[:, rows(t, P)], b[:, rows(t, P)], ACT.Exp, scale=-1.0,
                                                bias=b[:, (t + 1) * P - 1:(t + 1) * P])
                    if t < ST - 2:
                        step(last)
                give(act, last, edge_in, h + 1)
                for j in range(1, LEVELS):
                    act.wait_ge(t_ready, h * 7 + j)
                    e = H[:, j % 2, :].rearrange("p (n c) -> p n c", c=2 ** j)
                    half = 2 ** (j - 1)
                    step(nc.scalar.activation(e[:, :, 0:half], e[:, :, 0:half], ACT.Exp, scale=-1.0))
                    give(act, nc.scalar.activation(e[:, :, half:], e[:, :, half:], ACT.Exp), e_ready, h * 7 + j)
                act.wait_ge(cross_done, h + 1)
                give(act, nc.scalar.activation(W[:, 12:14, :].rearrange("p a c -> p (a c)")[:, 0:6 * P],
                                               ps[:, 2:4, :].rearrange("p a c -> p (a c)")[:, 0:6 * P], ACT.Copy),
                     cross_out, h + 1)
                norms[h].act(m, act)

        @block.gpsimd
        def _(pool):
            for h in range(HEADS):
                for j in range(1, LEVELS):
                    n = h * 7 + j
                    pool.wait_ge(e_ready, n)
                    if n > 2:
                        pool.wait_ge(level_done, h * LEVELS + j - 1 if j > 2 else h * LEVELS)
                    give(pool, nc.gpsimd.tensor_tensor(H[:, 4 + j % 2, :], W[:, h, :], H[:, j % 2, :], ALU.mult),
                         k_ready, n)

        @block.vector
        def _(dve):
            step = m.vlink.on(dve)

            def diff(h, j):
                b = A[:, 8 + h, :].rearrange("p (n c) -> p n c", c=2 ** j)
                half = 2 ** (j - 1)
                give(dve, nc.vector.tensor_tensor(H[:, j % 2, :].rearrange("p (n c) -> p n c", c=2 ** j), b,
                                                  b[:, :, half - 1:half].broadcast_to([P, S >> j, 2 ** j]),
                                                  ALU.subtract), t_ready, h * 7 + j)

            def take(h, j):
                n = h * LEVELS + j
                dve.wait_ge(level_done, n + 1)
                give(dve, nc.vector.copy_predicated(att, m.lvl[:, j:j + 1, :].broadcast_to([P, ST, P]),
                                                    tile4(ps[:, n % 2, :])), level_out, n + 1)

            for h in range(HEADS):
                q, k, b = A[:, h, :], W[:, h, :], A[:, 8 + h, :]
                diff(h, 1)
                step(nc.vector.memset(att, 0.0))
                take(h, 0)
                for j in range(1, LEVELS):
                    if j > 1:
                        dve.wait_ge(k_ready, h * 7 + j - 1)
                    if j + 1 < LEVELS:
                        diff(h, j + 1)
                    dve.wait_ge(e_ready, h * 7 + j)
                    give(dve, nc.vector.tensor_tensor(H[:, 2 + j % 2, :], q, H[:, j % 2, :], ALU.mult), q_ready,
                         h * 7 + j)
                    if j > 1:
                        take(h, j - 1)
                    if j == 1:
                        dve.wait_ge(edge_in, h + 1)
                        step(nc.vector.tensor_tensor(q1[:, P:], q[:, P:], eq[:, P:], ALU.mult))
                        step(nc.vector.tensor_tensor(k1[:, 0:3 * P], k[:, 0:3 * P], ek[:, 0:3 * P], ALU.mult))
                        step(nc.vector.tensor_scalar(ek[:, rows(3, P)], q1[:, rows(3, P)], eq[:, 3 * P - 1:3 * P],
                                                     None, ALU.mult))
                        give(dve, nc.vector.tensor_scalar(k0, k1[:, 0:P], eq[:, 2 * P - 1:2 * P], None, ALU.mult),
                             cross_in, h + 1)
                take(h, LEVELS - 1)
                dve.wait_ge(head_done, h + 1)
                give(dve, nc.vector.tensor_copy(q, ps[:, 6, :]), m.norm_in, norms[h].in_k)
                norms[h].dve(m, dve)
                step(nc.vector.scalar_tensor_tensor(q, q, m.p("h_norm", h), norms[h].std, ALU.mult, ALU.mult))
                step(nc.vector.tensor_tensor(q, q, A[:, 24 + h, :], ALU.mult))


def stage_route(m):
    nc, A, W, ps = m.nc, m.A, m.W, m.ps
    tok = lambda i: W[:, i, 0:ST * EXPERTS].rearrange("p (t e) -> p t e", e=EXPERTS)
    col = lambda i: m.small[:, rows(i, ST)]
    wide = lambda c: c.unsqueeze(2).broadcast_to([P, ST, EXPERTS])
    iota = m.c("iota").unsqueeze(1).broadcast_to([P, ST, EXPERTS])
    logits, l2, eq, one1, one2 = (tok(i) for i in range(5))
    top1, top2, at, w1, w2 = (col(i) for i in range(5))
    gT = W[0:EXPERTS, 6, :]
    scored, exp_in, exp_out, gate_in, gate_t, gate_rows, spread, spread_out = (m.sem("r_" + n) for n in (
        "logits", "exp_in", "exp", "gates", "gates_turned", "gate_rows", "spread", "spread_out"))
    with nc.Block() as block:
        @block.tensor
        def _(pe):
            for t in range(ST):
                for k in range(KD):
                    last = nc.tensor.matmul(ps[:, 4, rows(t, EXPERTS)], m.HN[:, k, rows(t, P)], m.rw[:, k, :],
                                            start=(k == 0), stop=(k == KD - 1))
            last.then_inc(scored, 1)
            pe.wait_ge(gate_in, 1)
            for t in range(ST):
                last = nc.tensor.transpose(ps[0:EXPERTS, 5, rows(t, P)], one1[:, t, :], m.c("ident"))
            last.then_inc(gate_t, 1)
            pe.wait_ge(gate_rows, 1)
            for e in range(EXPERTS):
                if e >= 2:
                    pe.wait_ge(spread_out, e - 1)
                nc.tensor.matmul(ps[:, 6 + e % 2, :], m.sel[:, e, :], gT, start=True, stop=True).then_inc(spread, 1)

        @block.scalar
        def _(act):
            act.wait_ge(exp_in, 1)
            give(act, nc.scalar.activation(w2, w2, ACT.Exp), exp_out, 1)
            for e in range(EXPERTS):
                act.wait_ge(spread, e + 1)
                give(act, nc.scalar.activation(A[:, e, :], ps[:, 6 + e % 2, :], ACT.Copy), spread_out, e + 1)

        @block.vector
        def _(dve):
            step = m.vlink.on(dve)
            dve.wait_ge(scored, 1)
            step(nc.vector.tensor_copy(logits, ps[:, 4, 0:ST * EXPERTS].rearrange("p (t e) -> p t e", e=EXPERTS)))

            def best(l, top, one):
                step(nc.vector.tensor_reduce(top, l, AX, ALU.max))
                step(nc.vector.tensor_tensor(eq, l, wide(top), ALU.is_equal))
                step(nc.vector.tensor_tensor(eq, eq, iota, ALU.mult))
                step(nc.vector.tensor_reduce(at, eq, AX, ALU.min))
                step(nc.vector.tensor_tensor(one, iota, wide(at), ALU.is_equal))

            best(logits, top1, one1)
            step(nc.vector.scalar_tensor_tensor(l2, one1, -BIG, logits, ALU.mult, ALU.add))
            best(l2, top2, one2)
            give(dve, nc.vector.tensor_tensor(w2, top2, top1, ALU.subtract), exp_in, 1)
            dve.wait_ge(exp_out, 1)
            step(nc.vector.tensor_scalar(w1, w2, 1.0, None, ALU.add))
            step(nc.vector.reciprocal(w1, w1))
            step(nc.vector.tensor_tensor(w2, w2, w1, ALU.mult))
            step(nc.vector.tensor_tensor(one1, one1, wide(w1), ALU.mult))
            step(nc.vector.tensor_tensor(one2, one2, wide(w2), ALU.mult))
            give(dve, nc.vector.tensor_tensor(one1, one1, one2, ALU.add), gate_in, 1)
            dve.wait_ge(gate_t, 1)
            give(dve, nc.vector.tensor_copy(gT, ps[0:EXPERTS, 5, :]), gate_rows, 1)


def stage_experts(m, a):
    nc, A, W, ps = m.nc, m.A, m.W, m.ps
    up, down = 2 * KE, KD
    total = up + down
    done = m.stream.done
    used = [len(range(s, total, SLOTS)) for s in range(SLOTS)]
    uses = list(m.stream.uses)
    silu, gated, hidden = m.sem("e_silu"), m.sem("e_gated"), m.sem("e_hidden")
    gate2 = gate_of(m, 1, 1)
    with nc.Block() as block:
        @block.sync
        def _(sp):
            with sp.Fori(0, EXPERTS) as e:
                for b in range(total):
                    s = b % SLOTS
                    prev = b - SLOTS if b >= SLOTS else (used[s] - 1) * SLOTS + s - total
                    sp.wait_ge(m.blocks_done, e * total + (done + prev + 1))
                    src = a["w_moe_up"][e * up + b] if b < up else a["w_moe_down"][e * down + (b - up)]
                    w = D if b < up else FFE
                    sp.dma_start(m.ring[:, s, 0:w], src).then_inc(m.loaded[s], 16)

        @block.tensor
        def _(pe):
            with pe.Fori(0, EXPERTS) as e:
                for b in range(total):
                    s = b % SLOTS
                    pe.wait_ge(m.loaded[s], e * (16 * used[s]) + 16 * (uses[s] + b // SLOTS + 1))
                    prev = b - BANKS if b >= BANKS else max(range(b, total, BANKS)) - total
                    pe.wait_ge(m.evac, e * total + (done + prev + 1))
                    kt, act = (KD, m.HN) if b < up else (KE, A[:, 8:8 + KE, :])
                    if b == up:
                        pe.wait_ge(hidden, e * KE + KE)
                    for k in range(kt):
                        last = nc.tensor.matmul(ps[:, b % BANKS, :], m.ring[:, s, rows(k, P)], act[:, k, :],
                                                start=(k == 0), stop=(k == kt - 1))
                    last.then_inc(m.blocks_done, 1)

        @block.scalar
        def _(act):
            with act.Fori(0, EXPERTS) as e:
                for j in range(KE):
                    act.wait_ge(m.blocks_done, e * total + (done + 2 * j + 1))
                    act.wait_ge(m.evac, e * total + (done + 2 * (j - 1) if j > 1 else done + 2 * (j - 1 + KE) - total))
                    nc.scalar.activation(W[:, j % 2, :], ps[:, 2 * j % BANKS, :], ACT.Silu).then_inc(silu, 1)

        @block.vector
        def _(dve):
            with dve.Fori(0, EXPERTS) as e:
                for j in range(KE):
                    dve.wait_ge(silu, e * KE + (j + 1))
                    dve.wait_ge(m.blocks_done, e * total + (done + 2 * j + 2))
                    t = W[:, 2 + j % 2, :]
                    nc.vector.tensor_tensor(t, W[:, j % 2, :], ps[:, (2 * j + 1) % BANKS, :],
                                            ALU.mult).then_inc(m.evac, 2)
                    dve.wait_ge(m.evac, e * total + (done + 2 * j + 2))
                    nc.vector.tensor_tensor(A[:, 8 + j:9 + j, :], t.unsqueeze(1), A[:, bass.ds(e, 1), :],
                                            ALU.mult).then_inc(hidden, 1)
                for d in range(KD):
                    b = up + d
                    dve.wait_ge(m.blocks_done, e * total + (done + b + 1))
                    nc.vector.scalar_tensor_tensor(m.X[:, d, :], ps[:, b % BANKS, :], gate2(d), m.X[:, d, :],
                                                   ALU.mult, ALU.add).then_inc(m.evac, 1)
                dve.wait_ge(m.evac, e * total + (done + total))


def stage_final(m, a):
    nc = m.nc
    norm = Norm(m, m.X[:], m.ones1024[:], m.W[:, 0:8, :], m.W[:, 8, :], m.c("eps6"), False, waits=False)
    ready = m.sem("out_ready")
    with nc.Block() as block:
        @block.tensor
        def _(pe):
            norm.pe(m, pe)

        @block.scalar
        def _(act):
            norm.act(m, act)

        @block.vector
        def _(dve):
            norm.dve(m, dve)
            for i in range(KD):
                nc.vector.scalar_tensor_tensor(m.HN[:, i, :], m.X[:, i, :], m.p("final", i), norm.std, ALU.mult,
                                               ALU.mult).then_inc(ready, 1)

        @block.sync
        def _(sp):
            for i in range(KD):
                sp.wait_ge(ready, i + 1)
                sp.dma_start(a["out"][:, i, :], m.HN[:, i, :]).then_inc(m.stored, 16)
            sp.wait_ge(m.stored, 16 * KD)


def program(nc, a):
    with ExitStack() as ctx:
        m = Chip(nc, ctx)
        m.stream = stream = Stream()
        m.plans = {name: stream.place(n, kt, a["w_" + name]) for name, n, kt in STREAM if "w_" + name in a}
        stage_setup(m, a)
        stage_project(m)
        stage_mix(m)
        stage_out(m)
        stage_ada(m)
        stage_modulate(m, 0, 0)
        stage_m_project(m)
        stage_m_heads(m)
        stage_residual(m, "m_out", m.A[:, 8:16, :], KD, gate_of(m, 0, 0), "ffn_up")
        stage_modulate(m, 0, 1)
        stage_ffn(m)
        stage_residual(m, "ffn_down", m.A, KE, gate_of(m, 0, 1), "h_in", halves=2)
        stage_modulate(m, 1, 0)
        stage_h_project(m)
        stage_h_heads(m)
        stage_residual(m, "h_out", m.A[:, 0:8, :], KD, gate_of(m, 1, 0), None)
        stage_modulate(m, 1, 1)
        stage_route(m)
        stage_experts(m, a)
        stage_final(m, a)



def by_tile(np, v):
    return v.reshape(-1, P).T


def weight_blocks(np, w):
    k, n = w.shape
    return w.reshape(k // P, P, n // P, P).transpose(2, 1, 0, 3).reshape(n // P, P, k)


def lay_out(np, i):
    f = lambda v: np.ascontiguousarray(v, dtype=np.float32)
    out = {"xT": i["x"][0].T.reshape(KD, P, S).transpose(1, 0, 2),
           "memT": i["mem"][0].T.reshape(KD, P, MEM).transpose(1, 0, 2)}
    row = lambda v: np.pad(v.reshape(HEADS, 1), ((0, P - HEADS), (0, 0)))
    vectors = {"conv_a": i["conv_a_w"], "sg_g": i["sg_ln_g"], "sg_b": i["sg_ln_b"], "pool_s": i["pool_scale"],
               "dw_w": i["cc_dw_w"], "dw_b": i["cc_dw_b"], "cc_g": i["cc_ln_g"], "cc_b": i["cc_ln_b"],
               "ln_g": i["ln_g"], "ln_b": i["ln_b"], "c": i["c_2"], "ada_b": i["ada_b_2"],
               "norm1": i["norm1_w_2"], "norm2": i["norm2_w_2"], "final": i["final_norm_w_2"],
               "m_conv_w": i["m_conv_w_2"], "m_conv_b": i["m_conv_b_2"], "m_norm": i["m_norm_w_2"],
               "lb": i["h_lb_logits_2"], "h_norm": i["h_norm_w_2"]}
    out["par"] = np.concatenate([by_tile(np, vectors[n]) if n in vectors else
                                 row(i["m_i_bias_2"] if n == "mi_b" else i["m_f_bias_2"]) for n, _ in PARAMS], 1)
    s, t = np.arange(P)[:, None], np.arange(P)[None, :]
    win = np.array([[2, 4], [8, 16]])[:, :, None].repeat(64, 2).reshape(2, P).T
    consts = {"ident": s == t, "tri": s <= t, "neg": np.where(s > t, -BIG, 0.0),
              "restart": np.broadcast_to(np.arange(S) % P != 0, (P, S)),
              "pinv": (1.0 / np.minimum(np.arange(16)[None, None, :] + 1, win[:, :, None])).reshape(P, 32),
              "pwin": 1.0 / win, "eps5": np.full((P, 1), 1e-5), "eps6": np.full((P, 1), 1e-6),
              "iota": np.broadcast_to(np.arange(EXPERTS) - EXPERTS, (P, EXPERTS)), "one": np.ones((P, 1))}
    out["cst"] = np.concatenate([consts[n].astype(np.float32) for n, _ in CONSTS], 1)
    lvl = [(s // (2 * b) == t // (2 * b)) & (s % (2 * b) < b) & (t % (2 * b) >= b) for b in (1, 2, 4, 8, 16, 32, 64)]
    out["lvl"] = np.ascontiguousarray(np.stack([s == t] + lvl, 1).astype(np.uint32))
    out["sel"] = np.repeat(np.eye(HEADS)[:, :, None], P, 2)
    out["sgw"] = i["sg_w"][0].transpose(2, 0, 1)
    out["sgb"] = i["sg_b"][0]
    out["plw"] = i["pool_w"][0]
    tiles = lambda w: w.reshape(-1, P, w.shape[1]).transpose(1, 0, 2)
    out["pw"] = tiles(i["cc_pw_w"][0])
    out["rw"] = tiles(i["moe_router_2"][0])
    m_in, up = i["m_w_in_2"][0], 2 * HEADS
    out["gw"] = tiles(m_in[:, -up:])
    order = [12, 13, 14, 15, 10, 11, 0, 1, 2, 3, 4, 5, 8, 9, 6, 7, 16, 17] + list(range(18, 28))
    out["w_in"] = weight_blocks(np, i["w_in"][0])[order]
    out["w_kv"] = weight_blocks(np, i["w_kv"][0])
    out["w_out"] = weight_blocks(np, i["w_out"][0])
    out["w_ada"] = np.concatenate([weight_blocks(np, w) for w in i["ada_w_2"]])
    out["w_m_in"] = weight_blocks(np, m_in[:, :-up])
    out["w_m_out"] = weight_blocks(np, i["m_w_out_2"][0])
    out["w_h_in"] = weight_blocks(np, i["h_w_in_2"][0])
    out["w_h_out"] = weight_blocks(np, i["h_w_out_2"][0])
    pair = lambda g, u: np.stack([weight_blocks(np, g), weight_blocks(np, u)], 1).reshape(-1, P, D)
    out["w_ffn_up"] = pair(i["ffn_w_gate_2"][0], i["ffn_w_up_2"][0])
    down = i["ffn_w_down_2"][0].reshape(2, KE, P, KD, P).transpose(3, 0, 2, 1, 4)
    out["w_ffn_down"] = down.reshape(2 * KD, P, FFE)
    out["w_moe_up"] = np.stack([pair(g, u) for g, u in zip(i["moe_w_gate_2"][0], i["moe_w_up_2"][0])]).reshape(-1, P, D)
    out["w_moe_down"] = np.stack([weight_blocks(np, w) for w in i["moe_w_down_2"][0]]).reshape(-1, P, FFE)
    return {n: v if v.dtype == np.uint32 else f(v) for n, v in out.items()}


def kernel(**inputs):
    import numpy as np
    import concourse.bacc as bacc
    from concourse.bass_utils import run_bass_kernel_spmd

    arrays = lay_out(np, {n: np.asarray(v) for n, v in inputs.items()})
    nc = bacc.Bacc("TRN2", target_bir_lowering=False, num_devices=1)
    a = {n: nc.dram_tensor("in_" + n, v.shape, mybir.dt.from_np(v.dtype), kind="ExternalInput").ap()
         for n, v in arrays.items()}
    a["out"] = nc.dram_tensor("out", (P, KD, S), F32, kind="ExternalOutput").ap()
    program(nc, a)
    r = run_bass_kernel_spmd(nc, [{"in_" + n: v for n, v in arrays.items()}], core_ids=[0])
    got = r.results[0]["out"]
    return np.ascontiguousarray(got.transpose(2, 1, 0)).reshape(1, S, D)
```

```python
from contextlib import ExitStack

import concourse.bass as bass
from concourse import mybir

F32 = mybir.dt.float32
U32 = mybir.dt.uint32
ALU = mybir.AluOpType
ACT = mybir.ActivationFunctionType
AX = mybir.AxisListType.X

P = 128
S = 512
ST = S // P
D = 1024
KD = D // P
DG = 256
MEM = 256
TAPS_A, TAPS_D, TAPS_M = 3, 31, 4
HEADS = 8
FF = 2816
FFE = FF // 2
KF = FF // P
KE = FFE // P
EXPERTS = 8
ALPHA = 2.0 ** 0.25
SLOTS = 8
SLOT = 11 * P
BANKS = 4
BIG = 1e30
COND = 1024
CHUNKS = 4
CAP = 192
PASSES = -(-S // CAP)
TAIL = CAP - P
ROWS = EXPERTS * CAP

PARAMS = [("conv_a", TAPS_A * 2), ("sg_g", 2), ("sg_b", 2), ("pool_s", 2), ("dw_w", TAPS_D * 2), ("dw_b", 2),
          ("cc_g", 2), ("cc_b", 2), ("ln_g", 8), ("ln_b", 8), ("c", 8), ("ada_b", 96), ("norm1", 16),
          ("norm2", 16), ("final", 8), ("m_conv_w", TAPS_M * 8), ("m_conv_b", 8), ("m_norm", 8),
          ("lb", 8), ("h_norm", 8), ("mi_b", 1), ("mf_b", 1)]
CONSTS = [("ident", P), ("tri", P), ("neg", P), ("restart", S), ("pinv", 32), ("pwin", 2), ("eps5", 1),
          ("eps6", 1), ("iota", EXPERTS), ("one", 1), ("before", P), ("first_row", EXPERTS), ("tok_id", ST)]
STREAM = [("kv", 4, KD), ("in", 28, KD), ("out", 8, 10), ("m_in", 24, KD), ("m_out", 8, KD),
          ("ffn_up", 2 * KF, KD), ("ffn_down", 16, KE), ("h_in", 32, KD), ("h_out", 8, KD)]


def columns(table):
    at, out = 0, {}
    for name, n in table:
        out[name] = (at, at + n)
        at += n
    return out, at


PCOL, NPAR = columns(PARAMS)
CCOL, NCST = columns(CONSTS)


class Link:

    def __init__(self, sem):
        self.sem, self.n = sem, 0

    def on(self, eng):
        def step(ins):
            self.n += 1
            ins.then_inc(self.sem, 1)
            eng.wait_ge(self.sem, self.n)
            return ins
        return step


class Stream:

    def __init__(self):
        self.uses, self.last, self.done = [0] * SLOTS, [0] * SLOTS, 0

    def place(self, n, kt, dram):
        plan = Plan()
        plan.n, plan.kt, plan.dram = n, kt, dram
        plan.done = self.done
        plan.uses = list(self.uses)
        plan.free = list(self.last)
        for b in range(n):
            self.uses[b % SLOTS] += 1
            self.last[b % SLOTS] = self.done + b + 1
        self.done += n
        return plan


class Plan:
    pass


def rows(i, n):
    return slice(i * n, (i + 1) * n)


class Chip:

    def __init__(self, nc, ctx):
        self.nc, self.ctx = nc, ctx
        sb = self.sb
        self.X = sb("x_res", [P, KD, S])
        self.HN = sb("x_norm", [P, KD, S])
        self.A = sb("act", [P, 32, S])
        self.W = sb("work", [P, 18, S])
        self.ring = sb("ring", [P, SLOTS, SLOT])
        self.par = sb("par", [P, NPAR])
        self.cst = sb("cst", [P, NCST])
        self.ones128 = sb("ones128", [P, P])
        self.ones256 = sb("ones256", [P, P])
        self.ones1024 = sb("ones1024", [P, P])
        self.ones = sb("ones", [P, P])
        self.lvl = sb("lvl", [P, 8, P], U32)
        self.sel = sb("sel", [HEADS, HEADS, P])
        self.sgw = sb("sgw", [P, 4, P])
        self.sgb = sb("sgb", [P, 2, P])
        self.plw = sb("plw", [P, 2, P])
        self.pw = sb("pw", [P, 2, DG])
        self.gw = sb("gw", [P, KD, 16])
        self.rw = sb("rw", [P, KD, EXPERTS])
        self.mod = sb("mod", [P, 96])
        self.cond = sb("cond", [P, KD])
        self.small = sb("small", [P, 64])
        self.table = sb("table", [P, 3 * ST + 2 * EXPERTS + 1], U32)
        self.zero = sb("zero", [EXPERTS, PASSES * CAP], U32)
        self.w12 = sb("w12", [P, 2 * ST])
        dram = lambda n, shape, dt=F32: nc.dram_tensor(n, shape, dt, kind="Internal").ap()
        self.d_tokens = dram("tokens_of_expert", (PASSES * ROWS, 1), U32)
        self.d_rows = dram("normed_rows", (S, D))
        self.d_result = dram("expert_rows", (PASSES * ROWS, D))
        self.ps = ctx.enter_context(nc.psum_tensor("banks", [P, 8, S], F32))
        self.loaded = [self.sem(f"slot{s}_loaded") for s in range(SLOTS)]
        self.blocks_done = self.sem("blocks_done")
        self.evac = self.sem("blocks_out")
        self.vlink, self.alink, self.glink, self.plink = (Link(self.sem(n)) for n in
                                                          ("dve_step", "act_step", "pool_step", "pe_step"))
        self.norm_in, self.norm_mean, self.norm_cent, self.norm_sq, self.norm_var, self.norm_std = (
            self.sem(n) for n in ("norm_in", "norm_mean", "norm_centred", "norm_squared", "norm_var", "norm_std"))
        self.norms = self.means = self.waited = 0
        self.stored = self.sem("stored")

    def sb(self, name, shape, dt=F32):
        return self.ctx.enter_context(self.nc.sbuf_tensor("sb_" + name, shape, dt))

    def sem(self, name):
        return self.ctx.enter_context(self.nc.semaphore(name))

    def p(self, name, i=None, n=1):
        a, b = PCOL[name]
        return self.par[:, a:b] if i is None else self.par[:, a + i:a + i + n]

    def c(self, name):
        a, b = CCOL[name]
        return self.cst[:, a:b]



def load_first(m, sp, plan):
    w = plan.kt * P
    for s in range(min(SLOTS, plan.n)):
        if plan.free[s]:
            sp.wait_ge(m.blocks_done, plan.free[s])
        sp.dma_start(m.ring[:, s, 0:w], plan.dram[s]).then_inc(m.loaded[s], 16)


def load_rest(m, sp, plan):
    w = plan.kt * P

    def load(b, s):
        sp.wait_ge(m.blocks_done, b + (plan.done + 1 - SLOTS))
        sp.dma_start(m.ring[:, s, 0:w], plan.dram[b]).then_inc(m.loaded[s], 16)

    turns = plan.n // SLOTS
    if turns > 1:
        with sp.Fori(1, turns) as i:
            for s in range(SLOTS):
                load(i * SLOTS + s, s)
    for b in range(max(turns, 1) * SLOTS, plan.n):
        load(b, b % SLOTS)


def product(m, pe, plan, block, loop=True, after=None):
    def one(b, s, use):
        pe.wait_ge(m.loaded[s], use * 16 + 16 * (plan.uses[s] + 1))
        out = b + (plan.done + 1 - BANKS)
        if not isinstance(out, int) or out > 0:
            pe.wait_ge(m.evac, out)
        block(m.ps[:, s % BANKS, :], m.ring[:, s, :]).then_inc(m.blocks_done, 1)

    turns = plan.n // SLOTS if loop else 0
    if turns:
        with pe.Fori(0, turns) as i:
            for s in range(SLOTS):
                one(i * SLOTS + s, s, i)
    for b in range(turns * SLOTS, plan.n):
        one(b, b % SLOTS, b // SLOTS)
        if after:
            after(b)


def by_features(m, act, kt):
    def block(bank, w):
        for k in range(kt):
            last = m.nc.tensor.matmul(bank[:, 0:act.shape[2]], w[:, rows(k, P)], act[:, k, :],
                                      start=(k == 0), stop=(k == kt - 1))
        return last
    return block


def by_tokens(m, act, kt, tiles):
    def block(bank, w):
        for t in range(tiles):
            for k in range(kt):
                last = m.nc.tensor.matmul(bank[:, rows(t, P)], act[:, k, rows(t, P)], w[:, rows(k, P)],
                                          start=(k == 0), stop=(k == kt - 1))
        return last
    return block



class Norm:

    def __init__(self, m, v, ones, sq, std, eps, centred, waits=True, bank=4):
        m.norms += 1
        m.means += centred
        m.waited += waits
        self.k, self.mean_k, self.in_k = m.norms, centred and m.means, waits and m.waited
        self.v, self.ones, self.sq, self.std, self.eps, self.bank = v, ones, sq, std, eps, bank
        self.n = v.shape[1]

    def pe(self, m, pe):
        bank, nt = m.ps[:, self.bank, :], self.n
        if self.mean_k:
            if self.in_k:
                pe.wait_ge(m.norm_in, self.in_k)
            for i in range(nt):
                last = m.nc.tensor.matmul(bank, self.ones, self.v[:, i, :], start=(i == 0), stop=(i == nt - 1))
            last.then_inc(m.norm_mean, 1)
        pe.wait_ge(m.norm_sq, self.k)
        bank = m.ps[:, self.bank + 1, :]
        for i in range(nt):
            last = m.nc.tensor.matmul(bank, self.ones, self.sq[:, i, :], start=(i == 0), stop=(i == nt - 1))
        last.then_inc(m.norm_var, 1)

    def act(self, m, act):
        self.square(m, act)
        self.root(m, act)

    def square(self, m, act):
        if self.mean_k:
            act.wait_ge(m.norm_cent, self.mean_k)
        elif self.in_k:
            act.wait_ge(m.norm_in, self.in_k)
        m.nc.scalar.activation(self.sq, self.v, ACT.Square).then_inc(m.norm_sq, 1)

    def root(self, m, act):
        act.wait_ge(m.norm_var, self.k)
        m.nc.scalar.activation(self.std, m.ps[:, self.bank + 1, :], ACT.Sqrt, bias=self.eps).then_inc(m.norm_std, 1)

    def dve(self, m, dve):
        if self.mean_k:
            dve.wait_ge(m.norm_mean, self.mean_k)
            mean = m.ps[:, self.bank, :].unsqueeze(1).broadcast_to([P, self.n, S])
            m.nc.vector.tensor_tensor(self.v, self.v, mean, ALU.subtract).then_inc(m.norm_cent, 1)
        dve.wait_ge(m.norm_std, self.k)
        m.vlink.on(dve)(m.nc.vector.reciprocal(self.std, self.std))

    def spread(self, n=None):
        return self.std.unsqueeze(1).broadcast_to([P, n or self.n, S])


def give(eng, ins, sem, count):
    ins.then_inc(sem, 1)
    eng.wait_ge(sem, count)



DA, DGT, XC, XA, BA, CA, V, U, Q, GATE = 0, 2, 4, 6, 8, 10, 12, 14, 16, 18
YA, YB, YC, YD, YE = 0, 2, 4, 6, 8


def stage_setup(m, a):
    nc = m.nc
    m.s_small, m.s_x, m.s_mem, m.s_gel, m.s_const = (m.sem(n) for n in ("small_loaded", "x_loaded", "mem_loaded",
                                                                        "table_loaded", "consts_set"))
    m.s_zero = m.sem("table_cleared")
    m.memT = m.W[:, 14:18, :].rearrange("p a (b c) -> p (a b) c", c=MEM)
    with nc.Block() as block:
        @block.sync
        def _(sp):
            sp.dma_start(m.memT, a["memT"]).then_inc(m.s_mem, 16)
            load_first(m, sp, m.plans["kv"])
            sp.dma_start(m.X[:], a["xT"]).then_inc(m.s_x, 16)

        @block.scalar
        def _(act):
            for out, src in ((m.par[:], a["par"]), (m.cst[:], a["cst"]), (m.lvl[:], a["lvl"]), (m.sel[:], a["sel"]),
                             (m.sgw[:], a["sgw"]), (m.plw[0:64, 0, 0:64], a["plw"][0]),
                             (m.plw[64:128, 0, 64:128], a["plw"][1]), (m.plw[0:64, 1, 0:64], a["plw"][2]),
                             (m.plw[64:128, 1, 64:128], a["plw"][3]), (m.pw[:], a["pw"]), (m.gw[:], a["gw"]),
                             (m.rw[:], a["rw"])):
                act.dma_start(out, src).then_inc(m.s_small, 16)
            for h in range(4):
                act.dma_start(m.sgb[64 * (h % 2):64 * (h % 2) + 64, h // 2, :],
                              a["sgb"][h].partition_broadcast(64)).then_inc(m.s_small, 16)
            m.n_small = 16 * 16
            act.wait_ge(m.s_small, m.n_small)
            nc.scalar.activation(m.cond[:], m.p("c"), ACT.Silu).then_inc(m.alink.sem, 1)
            m.alink.n += 1
            act.wait_ge(m.alink.sem, m.alink.n)

        @block.vector
        def _(dve):
            step = m.vlink.on(dve)
            for t, v in ((m.ones128, 1 / P), (m.ones256, 1 / DG), (m.ones1024, 1 / D), (m.ones, 1.0)):
                step(nc.vector.memset(t[:], v))

        @block.gpsimd
        def _(pool):
            step = m.glink.on(pool)
            for lo, j in ((0, 64), (64, 0)):
                step(nc.gpsimd.memset(m.plw[lo:lo + 64, :, j:j + 64], 0.0))
            step(nc.gpsimd.memset(m.zero[:], 0))
            pool.dma_start(m.d_tokens.rearrange("(e r) o -> e (r o)", e=EXPERTS), m.zero[:]).then_inc(m.s_zero, 16)
            pool.wait_ge(m.s_zero, 16)


def stage_project(m):
    nc, A, W = m.nc, m.A, m.W
    chunk = [W[:, 2 + 2 * i:4 + 2 * i, :].rearrange("p a c -> p (a c)") for i in range(CHUNKS)]
    sums = [m.HN[:, 2 * i:2 * i + 2, :].rearrange("p a c -> p (a c)") for i in range(2)]
    chunk_in, chunk_used = [m.sem(f"cond_loaded{i}") for i in range(CHUNKS)], m.sem("cond_used")
    acc_ready, acc_done = m.sem("cond_summed"), m.sem("cond_out")
    kv, inn, out = m.plans["kv"], m.plans["in"], m.plans["out"]
    m.kT, m.vm = A[:, 28, :].rearrange("p (j c) -> p j c", c=MEM), A[:, 29, :].rearrange("p (t c) -> p t c", c=DG)
    m.conv = W[:, 10:12, :]
    with nc.Block() as block:
        @block.sync
        def _(sp):
            load_first(m, sp, inn)
            load_rest(m, sp, inn)
            load_first(m, sp, out)

        @block.tensor
        def _(pe):
            pe.wait_ge(m.s_mem, 16)
            keys, values = by_features(m, m.memT, KD), by_tokens(m, m.memT, KD, 2)
            turn = iter((keys, keys, values, values))
            product(m, pe, kv, lambda bank, w: next(turn)(bank, w))
            pe.wait_ge(m.s_x, 16)

            def spread_sums(b):
                c = (b - 3) // 2
                if b < 3 or b % 2 == 0 or c >= 2 * 6 * D // COND:
                    return
                pe.wait_ge(acc_ready, c + 1)
                for j in range(COND // P):
                    last = nc.tensor.matmul(m.ps[:, 4 + c % 2, j:j + 1], sums[c % 2][:, rows(j, P)], m.ones[:, 0:1],
                                            start=True, stop=True)
                last.then_inc(acc_done, 1)
            product(m, pe, inn, by_features(m, m.X, KD), loop=False, after=spread_sums)

        @block.gpsimd
        def _(pool):
            for n in range(2 * 6 * KD * D // COND):
                if n >= CHUNKS:
                    pool.wait_ge(chunk_used, n - CHUNKS + 1)
                pool.dma_start(chunk[n % CHUNKS], m.cond_w[n]).then_inc(chunk_in[n % CHUNKS], 16)

        @block.scalar
        def _(act):
            step = m.alink.on(act)
            for b in range(4):
                act.wait_ge(m.blocks_done, kv.done + b + 1)
                if b < 2:
                    nc.scalar.activation(m.kT[:, b, :], m.ps[:, b, 0:MEM], ACT.Copy).then_inc(m.evac, 1)
                else:
                    nc.scalar.activation(m.vm[:, :, rows(b - 2, P)],
                                         m.ps[:, b, 0:2 * P].rearrange("p (t c) -> p t c", c=P),
                                         ACT.Copy).then_inc(m.evac, 1)
            for b in range(inn.n):
                act.wait_ge(m.blocks_done, inn.done + b + 1)
                how = (ACT.Sigmoid if DGT <= b < XC else ACT.Gelu_apprx_tanh if V <= b < Q else
                       ACT.Silu if b >= GATE else ACT.Copy)
                nc.scalar.activation(A[:, b, :], m.ps[:, b % BANKS, :], how).then_inc(m.evac, 1)

        @block.vector
        def _(dve):
            step = m.vlink.on(dve)
            ready = lambda tile: dve.wait_ge(m.evac, inn.done + tile)
            h = A[:, DA:DA + 2, :]
            nch = 2 * 6 * D // COND

            def conditioning(c):
                if c >= 2:
                    dve.wait_ge(acc_done, c - 1)
                    take(c - 2)
                for k in range(KD):
                    n = c * KD + k
                    dve.wait_ge(chunk_in[n % CHUNKS], 16 * (n // CHUNKS + 1))
                    src, out, w = chunk[n % CHUNKS], sums[c % 2], m.cond[:, k:k + 1]
                    give(dve, nc.vector.tensor_scalar(out, src, w, None, ALU.mult) if k == 0 else
                         nc.vector.scalar_tensor_tensor(out, src, w, out, ALU.mult, ALU.add), chunk_used, n + 1)
                give(dve, nc.vector.memset(m.small[:, 60:61], 0.0), acc_ready, c + 1)

            def take(c):
                n = COND // P
                step(nc.vector.tensor_tensor(m.mod[:, rows(c, n)], m.ps[:, 4 + c % 2, 0:n],
                                             m.p("ada_b")[:, rows(c, n)], ALU.add))

            def taps(first, last):
                for back in range(first, last):
                    for f in range(2):
                        acc = m.conv[:, f, back:]
                        step(nc.vector.scalar_tensor_tensor(acc, h[:, f, :S - back],
                                                            m.p("dw_w", 2 * (TAPS_D - 1 - back) + f), acc,
                                                            ALU.mult, ALU.add))

            for c in range(3):
                conditioning(c)
            ready(XC)
            step(nc.vector.tensor_tensor(h, h, A[:, DGT:DGT + 2, :], ALU.mult))
            for f in range(2):
                step(nc.vector.tensor_scalar(m.conv[:, f, :], h[:, f, :], m.p("dw_w", 2 * (TAPS_D - 1) + f),
                                             m.p("dw_b", f), ALU.mult, ALU.add))
            per = -(-(TAPS_D - 1) // (nch - 3))
            for c in range(3, nch):
                conditioning(c)
                taps(1 + per * (c - 3), min(1 + per * (c - 2), TAPS_D))
            ready(XA)
            x, s, d = A[:, XC:XC + 2, :], W[:, 12:14, :], A[:, 30:32, :]

            def double(out, src, back):
                step(nc.vector.tensor_copy(out[:, :, :back], src[:, :, :back]))
                step(nc.vector.tensor_tensor(out[:, :, back:], src[:, :, back:], src[:, :, :S - back], ALU.add))

            double(s, x, 1)
            double(d, s, 2)
            step(nc.vector.tensor_copy(s[64:128, 0:1, :], d[64:128, 0:1, :]))
            double(s[:, 1:2, :], d[:, 1:2, :], 4)
            double(d[64:128, 1:2, :], s[64:128, 1:2, :], 8)
            step(nc.vector.tensor_copy(s[64:128, 1:2, :], d[64:128, 1:2, :]))
            for f in range(2):
                step(nc.vector.tensor_scalar(s[:, f, 16:], s[:, f, 16:], m.c("pwin")[:, f:f + 1], None, ALU.mult))
                step(nc.vector.tensor_tensor(s[:, f, 0:16], s[:, f, 0:16], m.c("pinv")[:, rows(f, 16)], ALU.mult))
            step(nc.vector.tensor_tensor(s, s, x, ALU.subtract))
            ready(V)
            z, y = A[:, CA:CA + 2, :], W[:, YA:YA + 2, :]
            step(nc.vector.tensor_tensor(z, z, A[:, XA:XA + 2, :], ALU.mult))
            for f in range(2):
                step(nc.vector.tensor_scalar(y[:, f, :], z[:, f, :], m.p("conv_a", 2 * 2 + f), None, ALU.mult))
                for back in (1, 2):
                    acc = y[:, f, back:]
                    step(nc.vector.scalar_tensor_tensor(acc, z[:, f, :S - back], m.p("conv_a", 2 * (2 - back) + f),
                                                        acc, ALU.mult, ALU.add))
            step(nc.vector.tensor_tensor(y, y, A[:, BA:BA + 2, :], ALU.mult))
            for c in range(nch - 2, nch):
                dve.wait_ge(acc_done, c + 1)
                take(c)
            for layer in range(2):
                for half, w in ((0, "norm1"), (1, "norm2")):
                    at = layer * 48 + half * 24 + 8
                    step(nc.vector.tensor_scalar(m.mod[:, at:at + 8], m.mod[:, at:at + 8], 1.0, None, ALU.add))
                    step(nc.vector.tensor_tensor(m.mod[:, at:at + 8], m.mod[:, at:at + 8],
                                                 m.p(w, layer * 8, 8), ALU.mult))


def stage_mix(m):
    nc, A, W, ps = m.nc, m.A, m.W, m.ps
    v, u, vT = A[:, V:V + 2, :], A[:, U:U + 2, :], A[:, 30:32, :].rearrange("p a (b c) -> p (a b) c", c=DG)
    y = lambda j: W[:, j:j + 2, :]
    gated = lambda j: A[:, GATE + j:GATE + j + 2, :]
    sq, std, pooled = A[:, XC:XC + 2, :], A[:, XA, :], W[:, 12:14, :]
    prob = A[:, 2:4, :].rearrange("p a (b c) -> p (a b) c", c=MEM)
    prT = A[:, 0:2, :]
    norm_v = Norm(m, v, m.ones256[:], sq, std, m.c("eps5"), True, waits=False)
    norm_c = Norm(m, m.conv, m.ones256[:], sq, std, m.c("eps5"), True, waits=False)
    mx, nmx, rs, ri = (m.small[:, rows(i, 4)] for i in range(4))
    (vn_ready, vt_ready, vt_out, mixed, mixed_used, conv_ready, conv_act, pw_done, pool_done, score, score_top, probs,
     probs_scaled, pt_ready, pt_out, pv_done, masked, y_out) = (m.sem("mix_" + n) for n in (
         "v_normed", "v_turned", "v_turned_out", "gating", "gating_used", "conv_normed", "conv_silu", "pointwise",
         "pooled", "scores", "score_max", "exp", "probs", "probs_turned", "probs_turned_out", "attended", "masked",
         "attended_out"))
    with nc.Block() as block:
        @block.gpsimd
        def _(pool):
            for h in range(4):
                last = nc.gpsimd.tensor_tensor(m.sgw[:, h, :], m.sgw[:, h, :], m.c("tri"), ALU.mult)
                give(pool, last, masked, h + 1)

        @block.tensor
        def _(pe):
            norm_v.pe(m, pe)
            norm_c.pe(m, pe)
            pe.wait_ge(vn_ready, 1)
            for c in range(ST):
                for f in range(2):
                    last = nc.tensor.transpose(ps[:, 6 + c // 2, (c % 2) * DG + f * P:(c % 2) * DG + f * P + P],
                                               v[:, f, rows(c, P)], m.c("ident"))
            last.then_inc(vt_ready, 1)
            pe.wait_ge(vt_out, 1)
            pe.wait_ge(masked, 4)
            for h in range(4):
                lo = 64 * (h % 2)
                for c in range(ST):
                    last = nc.tensor.matmul(ps[lo:lo + 64, h // 2, rows(c, P)], vT[:, c, rows(h, 64)], m.sgw[:, h, :],
                                            start=True, stop=True)
            last.then_inc(mixed, 1)
            pe.wait_ge(conv_act, 1)
            for f in range(2):
                for k in range(2):
                    last = nc.tensor.matmul(ps[:, 2 + f, :], m.pw[:, k, rows(f, P)], m.conv[:, k, :],
                                            start=(k == 0), stop=(k == 1))
            last.then_inc(pw_done, 1)
            for f in range(2):
                last = nc.tensor.matmul(ps[:, 6 + f, :], m.plw[:, f, :], pooled[:, f, :], start=True, stop=True)
            last.then_inc(pool_done, 1)
            for h in range(4):
                lo = 64 * (h % 2)
                pe.wait_ge(mixed_used, 1 + 0 * h)
                if h:
                    pe.wait_ge(probs, h)
                for t in range(ST):
                    last = nc.tensor.matmul(ps[:, t // 2, rows(t % 2, MEM)], A[lo:lo + 64, Q + h // 2, rows(t, P)],
                                            m.kT[lo:lo + 64, h // 2, :], start=True, stop=True)
                last.then_inc(score, 1)
                pe.wait_ge(probs_scaled, h + 1)
                for k in range(2):
                    for t in range(ST):
                        last = nc.tensor.transpose(ps[:, 4 + k, rows(t, P)], prob[:, t, rows(k, P)], m.c("ident"))
                last.then_inc(pt_ready, 1)
                pe.wait_ge(pt_out, h + 1)
                if h == 0:
                    pe.wait_ge(y_out, 1)
                for k in range(2):
                    last = nc.tensor.matmul(ps[lo:lo + 64, 6 + h // 2, :], m.vm[:, k, rows(h, 64)], prT[:, k, :],
                                            start=(k == 0), stop=(k == 1))
                last.then_inc(pv_done, 1)

        @block.scalar
        def _(act):
            step = m.alink.on(act)
            norm_v.act(m, act)
            norm_c.act(m, act)
            act.wait_ge(vt_ready, 1)
            give(act, nc.scalar.activation(A[:, 30:32, :], ps[:, 6:8, :], ACT.Copy), vt_out, 1)
            act.wait_ge(conv_ready, 1)
            for f in range(2):
                last = nc.scalar.activation(m.conv[:, f, :], m.conv[:, f, :], ACT.Silu, bias=m.p("cc_b", f),
                                            scale=m.p("cc_g", f))
                if f == 0:
                    step(last)
            give(act, last, conv_act, 1)
            for h in range(4):
                act.wait_ge(score_top, h + 1)
                for t in range(ST):
                    last = nc.scalar.activation(prob[:, t, :], ps[:, t // 2, rows(t % 2, MEM)], ACT.Exp,
                                                bias=nmx[:, t:t + 1], scale=0.125, accum_out=rs[:, t:t + 1])
                    if t < ST - 1:
                        step(last)
                give(act, last, probs, h + 1)
                act.wait_ge(pt_ready, h + 1)
                give(act, nc.scalar.activation(prT, ps[:, 4:6, :], ACT.Copy), pt_out, h + 1)

        @block.vector
        def _(dve):
            step = m.vlink.on(dve)
            norm_v.dve(m, dve)
            step(nc.vector.tensor_tensor(v, v, norm_v.spread(), ALU.mult))
            step(nc.vector.tensor_scalar(v[:, 0, :], v[:, 0, :], m.p("sg_g", 0), m.p("sg_b", 0), ALU.mult, ALU.add))
            give(dve, nc.vector.tensor_scalar(v[:, 1, :], v[:, 1, :], m.p("sg_g", 1), m.p("sg_b", 1), ALU.mult,
                                              ALU.add), vn_ready, 1)
            norm_c.dve(m, dve)
            give(dve, nc.vector.tensor_tensor(m.conv, m.conv, norm_c.spread(), ALU.mult), conv_ready, 1)
            dve.wait_ge(mixed, 1)
            for f in range(2):
                step(nc.vector.tensor_tensor(W[:, YB + f, :].rearrange("p (c t) -> p c t", t=P),
                                             ps[:, f, :].rearrange("p (c t) -> p c t", t=P),
                                             m.sgb[:, f, :].unsqueeze(1).broadcast_to([P, ST, P]), ALU.add))
            step(nc.vector.tensor_tensor(y(YB), y(YB), u, ALU.mult))
            give(dve, nc.vector.tensor_tensor(y(YB), y(YB), gated(YB), ALU.mult), mixed_used, 1)
            step(nc.vector.tensor_tensor(y(YA), y(YA), gated(YA), ALU.mult))
            dve.wait_ge(pw_done, 1)
            step(nc.vector.tensor_tensor(y(YD), ps[:, 2:4, :], gated(YD), ALU.mult))
            dve.wait_ge(pool_done, 1)
            for f in range(2):
                last = nc.vector.scalar_tensor_tensor(W[:, YC + f, :], ps[:, 6 + f, :], m.p("pool_s", f),
                                                      A[:, GATE + YC + f, :], ALU.mult, ALU.mult)
                if f == 0:
                    step(last)
            give(dve, last, y_out, 1)
            for h in range(4):
                dve.wait_ge(score, h + 1)
                if h:
                    dve.wait_ge(probs, h)
                step(nc.vector.tensor_reduce(mx, ps[:, 0:2, :].rearrange("p a (b c) -> p (a b) c", c=MEM), AX,
                                             ALU.max))
                give(dve, nc.vector.tensor_scalar(nmx, mx, -0.125, None, ALU.mult), score_top, h + 1)
                dve.wait_ge(probs, h + 1)
                step(nc.vector.reciprocal(ri, rs))
                if h:
                    dve.wait_ge(pt_ready, h)
                give(dve, nc.vector.tensor_tensor(prob, prob, ri.unsqueeze(2).broadcast_to([P, ST, MEM]), ALU.mult),
                     probs_scaled, h + 1)
            dve.wait_ge(pv_done, 4)
            step(nc.vector.tensor_tensor(y(YE), ps[:, 6:8, :], gated(YE), ALU.mult))


def finish_norm_affine(m, dve, norm, scale, shift, out):
    nc, step = m.nc, m.vlink.on(dve)
    norm.dve(m, dve)
    for i in range(norm.n):
        step(nc.vector.scalar_tensor_tensor(out[:, i, :], norm.v[:, i, :], scale(i), norm.std, ALU.mult, ALU.mult))
        step(nc.vector.tensor_scalar(out[:, i, :], out[:, i, :], shift(i), None, ALU.add))


def stage_out(m):
    nc = m.nc
    plan = m.plans["out"]
    norm = Norm(m, m.X[:], m.ones1024[:], m.A[:, 0:8, :], m.A[:, 8, :], m.c("eps5"), True)
    with nc.Block() as block:
        @block.sync
        def _(sp):
            load_rest(m, sp, plan)
            load_first(m, sp, m.plans["m_in"])

        @block.tensor
        def _(pe):
            product(m, pe, plan, by_features(m, m.W[:, 0:10, :], 10))
            norm.pe(m, pe)

        @block.vector
        def _(dve):
            for b in range(plan.n):
                dve.wait_ge(m.blocks_done, plan.done + b + 1)
                nc.vector.scalar_tensor_tensor(m.X[:, b, :], m.X[:, b, :], ALPHA, m.ps[:, b % BANKS, :], ALU.mult,
                                               ALU.add).then_inc(m.evac, 1)
            dve.wait_ge(m.evac, plan.done + plan.n)
            give(dve, nc.vector.memset(m.small[:, 0:1], 0.0), m.norm_in, norm.in_k)
            finish_norm_affine(m, dve, norm, lambda i: m.p("ln_g", i), lambda i: m.p("ln_b", i), m.X)

        @block.scalar
        def _(act):
            norm.act(m, act)


def shift_of(m, layer, half):
    return lambda i: m.mod[:, layer * 48 + half * 24 + i:layer * 48 + half * 24 + i + 1]


def scale_of(m, layer, half):
    return lambda i: m.mod[:, layer * 48 + half * 24 + 8 + i:layer * 48 + half * 24 + 9 + i]


def gate_of(m, layer, half):
    return lambda i: m.mod[:, layer * 48 + half * 24 + 16 + i:layer * 48 + half * 24 + 17 + i]



def stage_modulate(m, layer, half):
    norm = Norm(m, m.X[:], m.ones1024[:], m.W[:, 0:8, :], m.W[:, 8, :], m.c("eps6"), False, waits=False)
    with m.nc.Block() as block:
        @block.tensor
        def _(pe):
            norm.pe(m, pe)

        @block.scalar
        def _(act):
            norm.act(m, act)

        @block.vector
        def _(dve):
            finish_norm_affine(m, dve, norm, scale_of(m, layer, half), shift_of(m, layer, half), m.HN)


def stage_m_project(m):
    nc, A, W, ps = m.nc, m.A, m.W, m.ps
    plan = m.plans["m_in"]
    m.g = {n: W[0:HEADS, 17 - j, :] for j, n in enumerate(("i", "f", "t", "m"))}
    g = m.g
    m.cT = W[:, 13, 0:ST * HEADS].rearrange("p (t h) -> p t h", h=HEADS)
    gates, gate_in, gate_soft, f_ready, em_in, conv_in, c_ready, cT_ready = (m.sem("m_" + n) for n in (
        "gates", "gate_rows", "gate_funcs", "forget", "floor_in", "conv_in", "decay", "decay_turned"))
    with nc.Block() as block:
        @block.sync
        def _(sp):
            load_rest(m, sp, plan)
            load_first(m, sp, m.plans["m_out"])

        @block.tensor
        def _(pe):
            for j in range(2):
                for k in range(KD):
                    last = nc.tensor.matmul(ps[0:HEADS, 4 + j, :], m.gw[:, k, rows(j, HEADS)], m.HN[:, k, :],
                                            start=(k == 0), stop=(k == KD - 1))
            last.then_inc(gates, 1)
            parts = by_features(m, m.HN, KD), by_tokens(m, m.HN, KD, ST)
            turn = iter([parts[0]] * 8 + [parts[1]] * 8 + [parts[0]] * 8)
            product(m, pe, plan, lambda bank, w: next(turn)(bank, w), loop=False)
            pe.wait_ge(c_ready, 1)
            for t in range(ST):
                last = nc.tensor.transpose(ps[:, 6, rows(t, HEADS)], g["i"][:, rows(t, P)],
                                           m.c("ident")[0:HEADS, 0:HEADS])
            last.then_inc(cT_ready, 1)

        @block.scalar
        def _(act):
            step = m.alink.on(act)
            act.wait_ge(gate_in, 1)
            step(nc.scalar.activation(g["i"], g["i"], ACT.Tanh, scale=1 / 15.0))
            step(nc.scalar.activation(g["t"], g["t"], ACT.Exp, scale=-1.0))
            give(act, nc.scalar.activation(g["t"], g["t"], ACT.Ln, bias=m.c("one")[0:HEADS, :]), gate_soft, 1)
            for b in range(plan.n):
                act.wait_ge(m.blocks_done, plan.done + b + 1)
                how = ACT.Sigmoid if b >= 16 else ACT.Copy
                nc.scalar.activation(A[:, b, :], ps[:, b % BANKS, :], how).then_inc(m.evac, 1)
                if b == 9:
                    act.wait_ge(conv_in, 1)
                if 9 <= b < 16:
                    act.wait_ge(conv_in, b - 8)
                    step(nc.scalar.activation(A[:, b - 9, :], A[:, b - 9, :], ACT.Silu, bias=m.p("m_conv_b", b - 9)))
            act.wait_ge(conv_in, 8)
            step(nc.scalar.activation(A[:, 7, :], A[:, 7, :], ACT.Silu, bias=m.p("m_conv_b", 7)))
            act.wait_ge(em_in, 1)
            step(nc.scalar.activation(g["f"], g["m"], ACT.Exp, scale=-1.0))

        @block.vector
        def _(dve):
            step = m.vlink.on(dve)
            dve.wait_ge(gates, 1)
            step(nc.vector.tensor_scalar(g["i"], ps[0:HEADS, 4, :], m.p("mi_b")[0:HEADS, :], None, ALU.add))
            step(nc.vector.tensor_scalar(g["f"], ps[0:HEADS, 5, :], m.p("mf_b")[0:HEADS, :], None, ALU.add))
            give(dve, nc.vector.scalar_tensor_tensor(g["t"], g["f"], -1.0, g["f"], ALU.mult, ALU.max), gate_in, 1)
            dve.wait_ge(gate_soft, 1)
            step(nc.vector.scalar_tensor_tensor(g["t"], g["f"], 0.0, g["t"], ALU.min, ALU.subtract))
            one = W[0:HEADS, 12, :]
            step(nc.vector.memset(one, 1.0))
            step(nc.vector.tensor_tensor_scan(out=g["m"], data0=one, data1=g["t"], initial=0.0, op0=ALU.mult,
                                              op1=ALU.add))
            give(dve, nc.vector.scalar_tensor_tensor(g["i"], g["i"], 15.0, g["m"], ALU.mult, ALU.subtract),
                 c_ready, 1)
            step(nc.vector.tensor_tensor_scan(out=g["t"], data0=one, data1=g["i"], initial=0.0, op0=ALU.mult,
                                              op1=ALU.max))
            give(dve, nc.vector.tensor_tensor(g["m"], g["m"], g["t"], ALU.add), em_in, 1)
            step(nc.vector.tensor_scalar(g["t"], g["t"], -1.0, None, ALU.mult))
            for b in range(8):
                dve.wait_ge(m.evac, plan.done + b + 1)
                x, y = W[:, b % 2, :], A[:, b, :]
                step(nc.vector.tensor_copy(x, y))
                step(nc.vector.tensor_scalar(y, x, m.p("m_conv_w", 8 * (TAPS_M - 1) + b), None, ALU.mult))
                for back in range(1, TAPS_M):
                    last = nc.vector.scalar_tensor_tensor(y[:, back:], x[:, :S - back],
                                                          m.p("m_conv_w", 8 * (TAPS_M - 1 - back) + b), y[:, back:],
                                                          ALU.mult, ALU.add)
                    if back < TAPS_M - 1:
                        step(last)
                give(dve, last, conv_in, b + 1)
            dve.wait_ge(cT_ready, 1)
            step(nc.vector.tensor_copy(m.cT, ps[:, 6, 0:ST * HEADS].rearrange("p (t h) -> p t h", h=HEADS)))


def stage_m_heads(m):
    nc, A, W, ps, g = m.nc, m.A, m.W, m.ps, m.g
    prob, dens, sq = W[:, 0:4, :], (W[:, 4, :], W[:, 11, :]), W[:, 5:6, :]
    dec = W[:, 6:10, :]
    spread, edge, decay, score, prob_ready, counted, summed = (m.sem("mh_" + n) for n in (
        "rows", "edge", "decay", "scores", "weights", "weight_sums", "values"))
    norms = [Norm(m, A[:, 8 + h:9 + h, :], m.ones128[:], sq, W[:, 10, :], m.c("eps6"), False, bank=4)
             for h in range(HEADS)]

    def totals(pe, h):
        pe.wait_ge(prob_ready, h + 1)
        if h:
            pe.wait_ge(m.norm_std, norms[h - 1].k)
        for bank in (6, 5):
            for i in range(ST):
                last = nc.tensor.matmul(ps[:, bank, i * P:], A[:, 8 + h, rows(i, P)] if bank == 5 else m.ones[:],
                                        prob[:, i, i * P:], start=(i == 0), stop=(i == ST - 1))
            last.then_inc(counted if bank == 6 else summed, 1)

    with nc.Block() as block:
        @block.tensor
        def _(pe):
            for h in range(HEADS):
                lo = 64 * (h % 2)
                if h:
                    pe.wait_ge(prob_ready, h)
                nc.tensor.matmul(ps[:, 4, :], m.sel[:, h, :], g["t"], start=True, stop=True)
                nc.tensor.matmul(ps[:, 7, :], m.sel[:, h, :], g["f"], start=True, stop=True).then_inc(spread, 1)
                for i in range(ST):
                    last = nc.tensor.matmul(ps[:, i, i * P:], A[lo:lo + 64, 4 + h // 2, rows(i, P)],
                                            A[lo:lo + 64, h // 2, i * P:], start=True, stop=True)
                last.then_inc(score, 1)
                if h:
                    totals(pe, h - 1)
                    norms[h - 1].pe(m, pe)
            totals(pe, HEADS - 1)
            norms[HEADS - 1].pe(m, pe)

        @block.scalar
        def _(act):
            step = m.alink.on(act)
            for h in range(HEADS):
                act.wait_ge(edge, h + 1)
                for i in range(ST):
                    c = m.cT[:, i, h:h + 1]
                    last = nc.scalar.activation(dec[:, i, rows(i, P)], dec[:, i, rows(i, P)], ACT.Exp, bias=c)
                    if i < ST - 1:
                        step(last)
                        step(nc.scalar.activation(dec[:, i, (i + 1) * P:], ps[:, 4, (i + 1) * P:], ACT.Exp, bias=c))
                give(act, last, decay, h + 1)
                if h:
                    norms[h - 1].act(m, act)
            norms[HEADS - 1].act(m, act)

        @block.vector
        def _(dve):
            step = m.vlink.on(dve)

            def divide(h):
                y, den = A[:, 8 + h, :], dens[h % 2]
                dve.wait_ge(counted, h + 1)
                step(nc.vector.scalar_tensor_tensor(den, ps[:, 6, :], -1.0, den, ALU.mult, ALU.max))
                step(nc.vector.tensor_tensor(den, den, ps[:, 6, :], ALU.max))
                step(nc.vector.reciprocal(den, den))
                dve.wait_ge(summed, h + 1)
                give(dve, nc.vector.tensor_tensor(y, ps[:, 5, :], den, ALU.mult), m.norm_in, norms[h].in_k)

            def finish(h):
                y = A[:, 8 + h, :]
                norms[h].dve(m, dve)
                step(nc.vector.scalar_tensor_tensor(y, y, m.p("m_norm", h), norms[h].std, ALU.mult, ALU.mult))
                step(nc.vector.tensor_tensor(y, y, A[:, 16 + h, :], ALU.mult))

            for h in range(HEADS):
                dve.wait_ge(spread, h + 1)
                step(nc.vector.tensor_copy(dens[h % 2], ps[:, 7, :]))
                for i in range(ST):
                    last = nc.vector.tensor_tensor(dec[:, i, rows(i, P)], ps[:, 4, rows(i, P)], m.c("neg"), ALU.add)
                    if i < ST - 1:
                        step(last)
                give(dve, last, edge, h + 1)
                if h:
                    divide(h - 1)
                dve.wait_ge(decay, h + 1)
                dve.wait_ge(score, h + 1)
                for i in range(ST):
                    last = nc.vector.scalar_tensor_tensor(prob[:, i, i * P:], ps[:, i, i * P:], 0.125,
                                                          dec[:, i, i * P:], ALU.mult, ALU.mult)
                    if i < ST - 1:
                        step(last)
                give(dve, last, prob_ready, h + 1)
                if h:
                    finish(h - 1)
            divide(HEADS - 1)
            finish(HEADS - 1)


def stage_residual(m, name, act_in, kt, gate, nxt, halves=1):
    nc, plan = m.nc, m.plans[name]
    with nc.Block() as block:
        @block.sync
        def _(sp):
            load_rest(m, sp, plan)
            if nxt:
                load_first(m, sp, m.plans[nxt])

        @block.tensor
        def _(pe):
            parts = [by_features(m, act_in[:, h * kt:(h + 1) * kt, :], kt) for h in range(halves)]
            turn = iter(parts * plan.n)
            product(m, pe, plan, lambda bank, w: next(turn)(bank, w))

        @block.vector
        def _(dve):
            step = m.vlink.on(dve)
            for b in range(plan.n):
                dve.wait_ge(m.blocks_done, plan.done + b + 1)
                x = m.X[:, b // halves, :]
                nc.vector.scalar_tensor_tensor(x, m.ps[:, b % BANKS, :], gate(b // halves), x, ALU.mult,
                                               ALU.add).then_inc(m.evac, 1)
                if halves > 1:
                    dve.wait_ge(m.evac, plan.done + b + 1)


def stage_ffn(m):
    nc, A, W, ps = m.nc, m.A, m.W, m.ps
    plan = m.plans["ffn_up"]
    silu, = (m.sem("ffn_silu"),)
    pairs = SLOTS // 2
    with nc.Block() as block:
        @block.sync
        def _(sp):
            load_rest(m, sp, plan)
            load_first(m, sp, m.plans["ffn_down"])

        @block.tensor
        def _(pe):
            product(m, pe, plan, by_features(m, m.HN, KD))

        turns, rest = divmod(plan.n // 2, pairs)

        @block.scalar
        def _(act):
            def one(j, s):
                act.wait_ge(m.blocks_done, j * 2 + (plan.done + 1))
                out = j * 2 + (plan.done - 2)
                act.wait_ge(m.evac, out)
                nc.scalar.activation(W[:, s % 2, :], ps[:, 2 * s % BANKS, :], ACT.Silu).then_inc(silu, 1)
            with act.Fori(0, turns) as i:
                for s in range(pairs):
                    one(i * pairs + s, s)
            for s in range(rest):
                one(turns * pairs + s, s)

        @block.vector
        def _(dve):
            def one(j, s):
                dve.wait_ge(silu, j + 1)
                dve.wait_ge(m.blocks_done, j * 2 + (plan.done + 2))
                out = A[:, bass.ds(j, 1), :] if not isinstance(j, int) else A[:, j:j + 1, :]
                nc.vector.tensor_tensor(out, W[:, s % 2:s % 2 + 1, :], ps[:, (2 * s + 1) % BANKS:(2 * s + 1) % BANKS + 1, :],
                                        ALU.mult).then_inc(m.evac, 2)
            with dve.Fori(0, turns) as i:
                for s in range(pairs):
                    one(i * pairs + s, s)
            for s in range(rest):
                one(turns * pairs + s, s)


LEVELS = 8
LN_EDGE = 2.0 ** -60
F_FLOOR = 1e-30
CROSS = [(0, 1), (2, 3), (1, 2), (1, 3), (0, 2), (0, 3)]


def stage_h_project(m):
    nc, A, W, ps = m.nc, m.A, m.W, m.ps
    plan = m.plans["h_in"]
    lb, oml, ex = m.small[:, 16:24], m.small[:, 24:32], m.small[:, 32:40]
    lb_in, lb_exp, both, log_in, log_out = (m.sem("h_" + n) for n in ("lb_in", "lb_exp", "sigmoids", "log_in", "logs"))
    with nc.Block() as block:
        @block.sync
        def _(sp):
            load_rest(m, sp, plan)
            load_first(m, sp, m.plans["h_out"])

        @block.tensor
        def _(pe):
            parts = by_features(m, m.HN, KD), by_tokens(m, m.HN, KD, ST)
            turn = iter([parts[0]] * 16 + [parts[1]] * 8 + [parts[0]] * 8)
            product(m, pe, plan, lambda bank, w: next(turn)(bank, w), loop=False)

        @block.scalar
        def _(act):
            step = m.alink.on(act)
            act.wait_ge(lb_in, 1)
            give(act, nc.scalar.activation(ex, ex, ACT.Exp), lb_exp, 1)
            for b in range(plan.n):
                act.wait_ge(m.blocks_done, plan.done + b + 1)
                bank = ps[:, b % BANKS, :]
                if 8 <= b < 16:
                    nc.scalar.activation(W[:, b - 8, :], bank, ACT.Sigmoid, scale=-1.0).then_inc(both, 1)
                    nc.scalar.activation(A[:, b, :], bank, ACT.Sigmoid).then_inc(m.evac, 1)
                else:
                    nc.scalar.activation(A[:, b, :], bank, ACT.Copy if 16 <= b < 24 else ACT.Silu).then_inc(m.evac, 1)
            for h in range(HEADS):
                act.wait_ge(log_in, h + 1)
                lo = W[:, 8 + h % 2, :]
                step(nc.scalar.activation(lo, lo, ACT.Ln, scale=1.0 / LN_EDGE))
                give(act, nc.scalar.activation(A[:, 8 + h, :], A[:, 8 + h, :], ACT.Ln), log_out, h + 1)

        @block.vector
        def _(dve):
            step = m.vlink.on(dve)
            give(dve, nc.vector.tensor_tensor(ex, m.p("lb"), m.p("lb"), ALU.subtract), lb_in, 1)
            dve.wait_ge(lb_exp, 1)
            step(nc.vector.reciprocal(oml, ex))
            step(nc.vector.tensor_tensor(ex, ex, oml, ALU.mult))
            step(nc.vector.tensor_tensor(lb, ex, ex, ALU.subtract))
            step(nc.vector.tensor_scalar(oml, lb, -1.0, 1.0, ALU.mult, ALU.add))

            def logs(h):
                dve.wait_ge(log_out, h + 1)
                f = A[:, 8 + h, :]
                step(nc.vector.tensor_tensor(f, f, W[:, 8 + h % 2, :], ALU.add))
                step(nc.vector.tensor_tensor_scan(out=W[:, 10, :], data0=m.c("restart"), data1=f, initial=0.0,
                                                  op0=ALU.mult, op1=ALU.add))
                step(nc.vector.tensor_copy(f, W[:, 10, :]))

            for h in range(HEADS):
                dve.wait_ge(m.evac, plan.done + 8 + h + 1)
                dve.wait_ge(both, h + 1)
                if h >= 2:
                    logs(h - 2)
                k, f, lo = W[:, h, :], A[:, 8 + h, :], W[:, 8 + h % 2, :]
                step(nc.vector.tensor_scalar(k, k, oml[:, h:h + 1], None, ALU.mult))
                step(nc.vector.tensor_scalar(f, f, oml[:, h:h + 1], lb[:, h:h + 1], ALU.mult, ALU.add))
                step(nc.vector.tensor_scalar(lo, f, F_FLOOR, LN_EDGE, ALU.max, ALU.min))
                give(dve, nc.vector.tensor_scalar(f, f, LN_EDGE, None, ALU.max), log_in, h + 1)
            for h in range(HEADS - 2, HEADS):
                logs(h)


def stage_h_heads(m):
    nc, A, W, ps, H = m.nc, m.A, m.W, m.ps, m.HN
    t_ready, e_ready, q_ready, k_ready, level_done, level_out, edge_in, cross_in, cross_done, cross_out, \
        head_done = (m.sem("hh_" + n) for n in (
            "diff", "decay", "q", "k", "level", "level_out", "edge_decay", "cross_in", "cross", "cross_out", "head"))
    tile4 = lambda t: t.rearrange("p (t c) -> p t c", c=P)
    atts = tile4(W[:, 11, :]), tile4(W[:, 9, :])
    cross = W[:, 12:14, :].rearrange("p a (t c) -> p (a t) c", c=P)
    eq, ek, q1, k1, k0 = W[:, 14, :], W[:, 15, :], W[:, 16, :], W[:, 17, :], W[:, 8, 0:P]
    norms = [Norm(m, A[:, h:h + 1, :], m.ones128[:], H[:, 6:7, :], H[:, 7, :], m.c("eps6"), False, bank=4)
             for h in range(HEADS)]
    VALUES, BETWEEN, NORMED = 3, 5, 6

    def values(pe, h):
        pe.wait_ge(level_out, (h + 1) * LEVELS)
        pe.wait_ge(cross_out, h + 1)
        for t in range(ST):
            parts = [(t, atts[h % 2][:, t, :])] + [(s, cross[:, i, :]) for i, (s, tt) in enumerate(CROSS) if tt == t]
            for i, (s, w) in enumerate(parts):
                last = nc.tensor.matmul(ps[:, 6, rows(t, P)], A[:, 16 + h, rows(s, P)], w, start=(i == 0),
                                        stop=(i == len(parts) - 1))
        last.then_inc(head_done, 1)

    def products(pe, h):
        pe.wait_ge(cross_in, h + 1)
        for i, (s, t) in enumerate(CROSS):
            lhs = k0 if s == 0 and t > 1 else k1[:, rows(s, P)]
            rhs = ek[:, rows(3, P)] if t == 3 and s < 2 else q1[:, rows(t, P)]
            last = nc.tensor.matmul(ps[:, 2 + i // 4, rows(i % 4, P)], lhs, rhs, start=True, stop=True)
        last.then_inc(cross_done, 1)

    with nc.Block() as block:
        @block.tensor
        def _(pe):
            for h in range(HEADS):
                q, k = A[:, h, :], W[:, h, :]
                for j in range(LEVELS):
                    n = h * LEVELS + j
                    if n >= 2:
                        pe.wait_ge(level_out, n - 1)
                    if j:
                        pe.wait_ge(q_ready, h * 7 + j)
                        pe.wait_ge(k_ready, h * 7 + j)
                    level = (h * 7 + j) % 2
                    lhs, rhs = (H[:, 4 + level, :], H[:, 2 + level, :]) if j else (k, q)
                    for t in range(ST):
                        last = nc.tensor.matmul(ps[:, n % 2, rows(t, P)], lhs[:, rows(t, P)], rhs[:, rows(t, P)],
                                                start=True, stop=True)
                    last.then_inc(level_done, 1)
                    if h and j == VALUES:
                        values(pe, h - 1)
                    if j == BETWEEN:
                        products(pe, h)
                    if h and j == NORMED:
                        norms[h - 1].pe(m, pe)
            values(pe, HEADS - 1)
            norms[HEADS - 1].pe(m, pe)

        @block.scalar
        def _(act):
            step = m.alink.on(act)

            def decays(h, j):
                n = h * 7 + j
                act.wait_ge(t_ready, n)
                e = H[:, n % 2, :].rearrange("p (n c) -> p n c", c=2 ** j)
                half = 2 ** (j - 1)
                step(nc.scalar.activation(e[:, :, 0:half], e[:, :, 0:half], ACT.Exp, scale=-1.0))
                give(act, nc.scalar.activation(e[:, :, half:], e[:, :, half:], ACT.Exp), e_ready, n)

            def take_cross(h):
                act.wait_ge(cross_done, h + 1)
                if h:
                    act.wait_ge(head_done, h)
                give(act, nc.scalar.activation(W[:, 12:14, :].rearrange("p a c -> p (a c)")[:, 0:6 * P],
                                               ps[:, 2:4, :].rearrange("p a c -> p (a c)")[:, 0:6 * P], ACT.Copy),
                     cross_out, h + 1)

            for h in range(HEADS):
                b = A[:, 8 + h, :]
                decays(h, 1)
                if h:
                    take_cross(h - 1)
                if h > 1:
                    norms[h - 2].root(m, act)
                decays(h, 2)
                step(nc.scalar.activation(eq[:, P:], b[:, P:], ACT.Exp))
                for t in range(ST - 1):
                    last = nc.scalar.activation(ek[:, rows(t, P)], b[:, rows(t, P)], ACT.Exp, scale=-1.0,
                                                bias=b[:, (t + 1) * P - 1:(t + 1) * P])
                    if t < ST - 2:
                        step(last)
                give(act, last, edge_in, h + 1)
                for j in range(3, LEVELS):
                    decays(h, j)
                    if h and j == NORMED:
                        norms[h - 1].square(m, act)
            take_cross(HEADS - 1)
            norms[HEADS - 2].root(m, act)
            norms[HEADS - 1].act(m, act)

        @block.gpsimd
        def _(pool):
            def diff(h, j):
                n = h * 7 + j
                if n > 2:
                    pool.wait_ge(q_ready, n - 2)
                b = A[:, 8 + h, :].rearrange("p (n c) -> p n c", c=2 ** j)
                half = 2 ** (j - 1)
                give(pool, nc.gpsimd.tensor_tensor(H[:, n % 2, :].rearrange("p (n c) -> p n c", c=2 ** j), b,
                                                   b[:, :, half - 1:half].broadcast_to([P, S >> j, 2 ** j]),
                                                   ALU.subtract), t_ready, n)

            diff(0, 1)
            for h in range(HEADS):
                for j in range(1, LEVELS):
                    n = h * 7 + j
                    if n < HEADS * 7:
                        diff(n // 7, n % 7 + 1)
                    pool.wait_ge(e_ready, n)
                    if n > 2:
                        pool.wait_ge(level_done, h * LEVELS + j - (1 if j > 2 else 2))
                    give(pool, nc.gpsimd.tensor_tensor(H[:, 4 + n % 2, :], W[:, h, :], H[:, n % 2, :], ALU.mult),
                         k_ready, n)

        @block.vector
        def _(dve):
            step = m.vlink.on(dve)

            def take(h, j):
                n = h * LEVELS + j
                dve.wait_ge(level_done, n + 1)
                give(dve, nc.vector.copy_predicated(atts[h % 2], m.lvl[:, j:j + 1, :].broadcast_to([P, ST, P]),
                                                    tile4(ps[:, n % 2, :])), level_out, n + 1)

            def take_values(h):
                dve.wait_ge(head_done, h + 1)
                give(dve, nc.vector.tensor_copy(A[:, h, :], ps[:, 6, :]), m.norm_in, norms[h].in_k)

            def finish(h, half):
                half = rows(half, S // 2)
                y, std = A[:, h, half], norms[h].std[:, half]
                dve.wait_ge(m.norm_std, norms[h].k)
                step(nc.vector.reciprocal(std, std))
                step(nc.vector.scalar_tensor_tensor(y, y, m.p("h_norm", h), std, ALU.mult, ALU.mult))
                step(nc.vector.tensor_tensor(y, y, A[:, 24 + h, half], ALU.mult))

            def times(h, j):
                n = h * 7 + j
                dve.wait_ge(e_ready, n)
                give(dve, nc.vector.tensor_tensor(H[:, 2 + n % 2, :], A[:, h, :], H[:, n % 2, :], ALU.mult), q_ready, n)

            for h in range(HEADS):
                q, k = A[:, h, :], W[:, h, :]
                times(h, 1)
                if h:
                    take(h - 1, LEVELS - 1)
                step(nc.vector.memset(atts[h % 2], 0.0))
                take(h, 0)
                for j in range(1, LEVELS):
                    if j > 1:
                        times(h, j)
                        take(h, j - 1)
                    if h > 1 and j <= 2:
                        finish(h - 2, j - 1)
                    if j == 4:
                        dve.wait_ge(edge_in, h + 1)
                        step(nc.vector.tensor_tensor(q1[:, P:], q[:, P:], eq[:, P:], ALU.mult))
                        step(nc.vector.tensor_tensor(k1[:, 0:3 * P], k[:, 0:3 * P], ek[:, 0:3 * P], ALU.mult))
                        step(nc.vector.tensor_scalar(ek[:, rows(3, P)], q1[:, rows(3, P)], eq[:, 3 * P - 1:3 * P],
                                                     None, ALU.mult))
                        give(dve, nc.vector.tensor_scalar(k0, k1[:, 0:P], eq[:, 2 * P - 1:2 * P], None, ALU.mult),
                             cross_in, h + 1)
                    if h and j == VALUES + 2:
                        take_values(h - 1)
            take(HEADS - 1, LEVELS - 1)
            for half in range(2):
                finish(HEADS - 2, half)
            take_values(HEADS - 1)
            for half in range(2):
                finish(HEADS - 1, half)


def stage_route(m):
    nc, A, W, ps = m.nc, m.A, m.W, m.ps
    tok = lambda i: W[:, i, 0:ST * EXPERTS].rearrange("p (t e) -> p t e", e=EXPERTS)
    col = lambda i: m.small[:, rows(i, ST)]
    wide = lambda c: c.unsqueeze(2).broadcast_to([P, ST, EXPERTS])
    over = lambda n: m.c(n).unsqueeze(1).broadcast_to([P, ST, EXPERTS])
    logits, l2, eq, one1, one2, both, place = (tok(i) for i in range(7))
    top1, top2, at, slot1, slot2 = (col(i) for i in range(5))
    most = m.small[:, 20:21]
    w1, w2 = m.w12[:, 0:ST], m.w12[:, ST:2 * ST]
    turned = W[:, 8:16, :].rearrange("p (t a) c -> p t (a c)", t=ST)
    scored, exp_in, exp_out, chosen, placed, tables, scattered, row_ready, row_out, row_stored = (
        m.sem("r_" + n) for n in ("logits", "exp_in", "exp", "chosen", "ranks", "tables", "scattered", "row_turned",
                                  "row_out", "row_stored"))
    with nc.Block() as block:
        @block.tensor
        def _(pe):
            for t in range(ST):
                for k in range(KD):
                    last = nc.tensor.matmul(ps[:, 4, rows(t, EXPERTS)], m.HN[:, k, rows(t, P)], m.rw[:, k, :],
                                            start=(k == 0), stop=(k == KD - 1))
            last.then_inc(scored, 1)
            for t in range(ST):
                if t >= 2:
                    pe.wait_ge(row_out, t - 1)
                for k in range(KD):
                    last = nc.tensor.transpose(ps[:, 2 * (t % 2) + k // 4, rows(k % 4, P)], m.HN[:, k, rows(t, P)],
                                               m.c("ident"))
                last.then_inc(row_ready, 1)
            pe.wait_ge(chosen, 1)
            for t in range(ST):
                for s in range(t + 1):
                    nc.tensor.matmul(ps[:, 5, rows(t, EXPERTS)], m.c("before") if s == t else m.ones[:],
                                     both[:, s, :], start=(s == 0), stop=(s == t))
            for s in range(ST):
                last = nc.tensor.matmul(ps[:, 5, rows(ST, EXPERTS)], m.ones[:], both[:, s, :], start=(s == 0),
                                        stop=(s == ST - 1))
            last.then_inc(placed, 1)

        @block.scalar
        def _(act):
            for t in range(ST):
                act.wait_ge(row_ready, t + 1)
                give(act, nc.scalar.activation(turned[:, t, :].rearrange("p (a c) -> p a c", c=S),
                                               ps[:, 2 * (t % 2):2 * (t % 2) + 2, :], ACT.Copy), row_out, t + 1)
                act.dma_start(m.d_rows[rows(t, P), :], turned[:, t, :]).then_inc(row_stored, 16)
            act.wait_ge(exp_in, 1)
            give(act, nc.scalar.activation(w2, w2, ACT.Exp), exp_out, 1)
            act.wait_ge(row_stored, 16 * ST)

        @block.gpsimd
        def _(pool):
            pool.wait_ge(tables, 1)
            for j in range(2):
                for t in range(ST):
                    nc.gpsimd.indirect_dma_start(
                        m.d_tokens, bass.IndirectOffsetOnAxis(ap=m.table[:, j * ST + t:j * ST + t + 1], axis=0),
                        m.table[:, 2 * ST + t:2 * ST + t + 1], None).then_inc(scattered, 16)
            pool.wait_ge(scattered, 16 * 2 * ST)

        @block.vector
        def _(dve):
            step = m.vlink.on(dve)
            dve.wait_ge(scored, 1)
            step(nc.vector.tensor_copy(logits, ps[:, 4, 0:ST * EXPERTS].rearrange("p (t e) -> p t e", e=EXPERTS)))

            def best(l, top, one):
                step(nc.vector.tensor_reduce(top, l, AX, ALU.max))
                step(nc.vector.tensor_tensor(eq, l, wide(top), ALU.is_equal))
                step(nc.vector.tensor_tensor(eq, eq, over("iota"), ALU.mult))
                step(nc.vector.tensor_reduce(at, eq, AX, ALU.min))
                step(nc.vector.tensor_tensor(one, over("iota"), wide(at), ALU.is_equal))

            best(logits, top1, one1)
            step(nc.vector.scalar_tensor_tensor(l2, one1, -BIG, logits, ALU.mult, ALU.add))
            best(l2, top2, one2)
            give(dve, nc.vector.tensor_tensor(both, one1, one2, ALU.add), chosen, 1)
            give(dve, nc.vector.tensor_tensor(w2, top2, top1, ALU.subtract), exp_in, 1)
            dve.wait_ge(exp_out, 1)
            step(nc.vector.tensor_scalar(w1, w2, 1.0, None, ALU.add))
            step(nc.vector.reciprocal(w1, w1))
            step(nc.vector.tensor_tensor(w2, w2, w1, ALU.mult))
            dve.wait_ge(placed, 1)
            ranks = ps[:, 5, 0:(ST + 1) * EXPERTS].rearrange("p (t e) -> p t e", e=EXPERTS)
            step(nc.vector.tensor_tensor(place, ranks[:, 0:ST, :], over("first_row"), ALU.add))
            for n in range(1, PASSES):
                step(nc.vector.tensor_scalar(eq, ranks[:, 0:ST, :], float(n * CAP), float(ROWS - CAP), ALU.is_ge,
                                             ALU.mult))
                step(nc.vector.tensor_tensor(place, place, eq, ALU.add))
            for one, slot in ((one1, slot1), (one2, slot2)):
                step(nc.vector.tensor_tensor(one, one, place, ALU.mult))
                step(nc.vector.tensor_reduce(slot, one, AX, ALU.add))
            step(nc.vector.tensor_reduce(most, ranks[:, ST, :], AX, ALU.max))
            step(nc.vector.tensor_copy(m.table[:, 3 * ST + 2 * EXPERTS:], most))
            step(nc.vector.tensor_copy(m.table[:, 2 * ST:3 * ST], m.c("tok_id")))
            give(dve, nc.vector.tensor_copy(m.table[:, 0:2 * ST], m.small[:, 3 * ST:5 * ST]), tables, 1)


def stage_experts(m, a):
    nc, A, W, ps = m.nc, m.A, m.W, m.ps
    up, down = 2 * KE, KD
    total = up + down
    done = m.stream.done
    used = [len(range(s, total, SLOTS)) for s in range(SLOTS)]
    uses = list(m.stream.uses)
    per_pass = EXPERTS * total
    rows_of = lambda i: m.table[:, 3 * ST + i * EXPERTS:3 * ST + (i + 1) * EXPERTS]
    most = m.table[0:1, 3 * ST + 2 * EXPERTS:3 * ST + 2 * EXPERTS + 1]
    tokens = m.d_tokens.rearrange("(p e r) o -> p r (e o)", e=EXPERTS, r=CAP)
    order = m.sem("e_order")
    BUFS = 4
    got = [(W[:, 4 * i:4 * i + 2, :].rearrange("p a c -> p (a c)"),
            W[0:TAIL, 4 * i + 2:4 * i + 4, :].rearrange("p a c -> p (a c)")) for i in range(BUFS)]
    three = lambda t: t.rearrange("p a c -> p (a c)").rearrange("p (k c) -> p k c", c=CAP)
    flat = A[:].rearrange("p a c -> p (a c)")
    hid = flat[:, 24 * S:24 * S + KE * CAP].rearrange("p (k c) -> p k c", c=CAP)
    yT = three(A[:, 29:32, :])
    silu_t = [W[:, 16 + i, 0:CAP] for i in range(2)]
    out_rows = [m.HN[:, 0:2, :], m.HN[0:TAIL, 2:4, :]]
    idx_in, got_in, turned, turned_out, silu, hidden, y_out, y_turned, y_rows, y_stored, gathers = (
        m.sem("e_" + n) for n in ("rows_in", "gathered", "turned", "turned_out", "silu", "hidden", "y", "y_turned",
                                  "y_rows", "y_stored", "pass_done"))
    got_sem = [m.sem(f"e_gathered{i}") for i in range(BUFS)]

    def passes(eng, body):
        body(0)
        n = eng.value_load(most, min_val=0, max_val=S)
        with eng.If(n > CAP):
            with eng.Fori(1, PASSES) as p:
                body(p)

    with nc.Block() as block:
        @block.gpsimd
        def _(pool):
            def body(p):
                if not isinstance(p, int):
                    pool.wait_ge(y_stored, p * (32 * EXPERTS) + 16)
                pool.dma_start(rows_of(0), tokens[p, 0:P, :],
                               allow_slow_non_contiguous=True).then_inc(idx_in, 16)
                pool.dma_start(rows_of(1)[0:TAIL, :], tokens[p, P:CAP, :],
                               allow_slow_non_contiguous=True).then_inc(idx_in, 16)
                pool.wait_ge(idx_in, p * 32 + 32)
                pool.sem_inc(order, 1)
                for e in range(EXPERTS):
                    if e >= BUFS:
                        pool.wait_ge(turned, p * EXPERTS + (e - BUFS + 1))
                        pool.sem_inc(order, 1)
                    for i, n in ((0, P), (1, TAIL)):
                        nc.gpsimd.indirect_dma_start(
                            got[e % BUFS][i], None, m.d_rows,
                            bass.IndirectOffsetOnAxis(ap=rows_of(i)[0:n, e:e + 1], axis=0)
                        ).then_inc(got_sem[e % BUFS], 16)
            passes(pool, body)

        @block.sync
        def _(sp):
            def body(p):
                with sp.Fori(0, EXPERTS) as e:
                    for b in range(total):
                        s = b % SLOTS
                        prev = b - SLOTS if b >= SLOTS else (used[s] - 1) * SLOTS + s - total
                        sp.wait_ge(m.blocks_done, p * per_pass + e * total + (done + prev + 1))
                        src = a["w_moe_up"][e * up + b] if b < up else a["w_moe_down"][e * down + (b - up)]
                        w = D if b < up else FFE
                        sp.dma_start(m.ring[:, s, 0:w], src).then_inc(m.loaded[s], 16)
            passes(sp, body)

        @block.tensor
        def _(pe):
            def body(p):
                for e in range(EXPERTS):
                    pe.wait_ge(got_sem[e % BUFS], p * (32 * (EXPERTS // BUFS)) + 32 * (e // BUFS + 1))
                    if not isinstance(p, int) or e:
                        pe.wait_ge(turned_out, p * EXPERTS + e)
                    for k in range(KD):
                        bank, col = 4 + k // 2, (k % 2) * CAP
                        nc.tensor.transpose(ps[:, bank, col:col + P], got[e % BUFS][0][:, rows(k, P)], m.c("ident"))
                        last = nc.tensor.transpose(ps[:, bank, col + P:col + CAP], got[e % BUFS][1][:, rows(k, P)],
                                                   m.c("ident")[0:TAIL, 0:TAIL])
                    last.then_inc(turned, 1)
                pe.wait_ge(turned_out, p * EXPERTS + EXPERTS)
                pe.sem_inc(order, 1)
                with pe.Fori(0, EXPERTS) as e:
                    for b in range(total):
                        s = b % SLOTS
                        pe.wait_ge(m.loaded[s], p * (16 * used[s] * EXPERTS) + e * (16 * used[s]) +
                                   16 * (uses[s] + b // SLOTS + 1))
                        prev = b - BANKS if b >= BANKS else max(range(b, total, BANKS)) - total
                        pe.wait_ge(m.evac, p * per_pass + e * total + (done + prev + 1))
                        kt = KD if b < up else KE
                        if b == up:
                            pe.wait_ge(hidden, p * (KE * EXPERTS) + e * KE + KE)
                        for k in range(kt):
                            act = flat[:, bass.ds(e * (3 * S) + k * CAP, CAP)] if b < up else hid[:, k, :]
                            last = nc.tensor.matmul(ps[:, b % BANKS, 0:CAP], m.ring[:, s, rows(k, P)], act,
                                                    start=(k == 0), stop=(k == kt - 1))
                        last.then_inc(m.blocks_done, 1)
                    pe.wait_ge(m.evac, p * per_pass + e * total + (done + total))
                    pe.wait_ge(turned_out, p * EXPERTS + EXPERTS)
                    pe.wait_ge(y_rows, p * EXPERTS + e + 1)
                    for k in range(KD):
                        nc.tensor.transpose(ps[:, 4 + k // 4, rows(k % 4, P)], yT[:, k, 0:P], m.c("ident"))
                        last = nc.tensor.transpose(ps[0:TAIL, 6 + k // 4, rows(k % 4, P)], yT[:, k, P:CAP],
                                                   m.c("ident"))
                    last.then_inc(y_turned, 1)
            passes(pe, body)

        @block.scalar
        def _(act):
            def body(p):
                for e in range(EXPERTS):
                    act.wait_ge(turned, p * EXPERTS + (e + 1))
                    give(act, nc.scalar.activation(
                        flat[:, 3 * S * e:3 * S * (e + 1)].rearrange("p (b c) -> p b c", c=2 * CAP),
                        ps[:, 4:8, 0:2 * CAP], ACT.Copy), turned_out, p * EXPERTS + (e + 1))
                with act.Fori(0, EXPERTS) as e:
                    base = p * per_pass + e * total
                    for j in range(KE):
                        act.wait_ge(m.blocks_done, base + (done + 2 * j + 1))
                        act.wait_ge(m.evac, base + (done + 2 * (j - 1) if j > 1 else done + 2 * (j - 1 + KE) - total))
                        nc.scalar.activation(silu_t[j % 2], ps[:, 2 * j % BANKS, 0:CAP], ACT.Silu).then_inc(silu, 1)
                    for d in range(down):
                        b = up + d
                        act.wait_ge(m.blocks_done, base + (done + b + 1))
                        nc.scalar.activation(yT[:, d, :], ps[:, b % BANKS, 0:CAP], ACT.Copy).then_inc(m.evac, 1)
                    act.wait_ge(y_turned, p * EXPERTS + e + 1)
                    act.wait_ge(y_stored, p * (32 * EXPERTS) + e * 32 + 16)
                    nc.scalar.activation(out_rows[0], ps[:, 4:6, :], ACT.Copy).then_inc(y_out, 1)
                    nc.scalar.activation(out_rows[1], ps[0:TAIL, 6:8, :], ACT.Copy).then_inc(y_rows, 1)
                    act.wait_ge(y_out, p * EXPERTS + e + 1)
                    act.wait_ge(y_rows, p * EXPERTS + e + 2)
                    row = p * (EXPERTS * CAP) + e * CAP
                    for i, n, at in ((0, P, 0), (1, TAIL, P)):
                        act.dma_start(m.d_result[bass.ds(row + at, n), :],
                                      out_rows[i].rearrange("p a c -> p (a c)")).then_inc(y_stored, 16)
                act.wait_ge(y_stored, p * (32 * EXPERTS) + (32 * EXPERTS + 16))
            act.sem_inc(y_rows, 1)
            act.sem_inc(y_stored, 16)
            passes(act, body)

        @block.vector
        def _(dve):
            def body(p):
                with dve.Fori(0, EXPERTS) as e:
                    base = p * per_pass + e * total
                    for j in range(KE):
                        dve.wait_ge(silu, p * (KE * EXPERTS) + e * KE + (j + 1))
                        dve.wait_ge(m.blocks_done, base + (done + 2 * j + 2))
                        nc.vector.tensor_tensor(hid[:, j, :], silu_t[j % 2], ps[:, (2 * j + 1) % BANKS, 0:CAP],
                                                ALU.mult).then_inc(m.evac, 2)
                        dve.wait_ge(m.evac, base + (done + 2 * j + 2))
                        dve.sem_inc(hidden, 1)
            passes(dve, body)


def stage_combine(m):
    nc, A, W, ps = m.nc, m.A, m.W, m.ps
    gate2 = gate_of(m, 1, 1)
    row = lambda i: A[:, 2 * i:2 * i + 2, :].rearrange("p a c -> p (a c)")
    gathered, mixed, turned = [m.sem(f"c_gathered{t}") for t in range(ST)], m.sem("c_mixed"), m.sem("c_turned")
    with nc.Block() as block:
        @block.gpsimd
        def _(pool):
            def gather(table):
                for t in range(ST):
                    for j in range(2):
                        nc.gpsimd.indirect_dma_start(
                            row(2 * t + j), None, table,
                            bass.IndirectOffsetOnAxis(ap=m.table[:, j * ST + t:j * ST + t + 1], axis=0)
                        ).then_inc(gathered[t], 16)
            most = m.table[0:1, 3 * ST + 2 * EXPERTS:3 * ST + 2 * EXPERTS + 1]
            n = pool.value_load(most, min_val=0, max_val=S)
            with pool.If(n > CAP):
                gather(m.d_result)
            with pool.If(n <= CAP):
                gather(m.d_result[0:ROWS, :])

        @block.vector
        def _(dve):
            step = m.vlink.on(dve)
            for t in range(ST):
                dve.wait_ge(gathered[t], 32)
                a1, a2 = row(2 * t), row(2 * t + 1)
                step(nc.vector.tensor_scalar(a1, a1, m.w12[:, t:t + 1], None, ALU.mult))
                give(dve, nc.vector.scalar_tensor_tensor(a1, a2, m.w12[:, ST + t:ST + t + 1], a1, ALU.mult, ALU.add),
                     mixed, t + 1)
            dve.wait_ge(turned, 1)
            for k in range(KD):
                step(nc.vector.scalar_tensor_tensor(m.X[:, k, :], ps[:, k, :], gate2(k), m.X[:, k, :], ALU.mult,
                                                    ALU.add))

        @block.tensor
        def _(pe):
            for t in range(ST):
                pe.wait_ge(mixed, t + 1)
                for k in range(KD):
                    last = nc.tensor.transpose(ps[:, k, rows(t, P)], row(2 * t)[:, rows(k, P)], m.c("ident"))
            last.then_inc(turned, 1)


def stage_final(m, a):
    nc = m.nc
    norm = Norm(m, m.X[:], m.ones1024[:], m.W[:, 0:8, :], m.W[:, 8, :], m.c("eps6"), False, waits=False)
    ready = m.sem("out_ready")
    with nc.Block() as block:
        @block.tensor
        def _(pe):
            norm.pe(m, pe)

        @block.scalar
        def _(act):
            norm.act(m, act)

        @block.vector
        def _(dve):
            norm.dve(m, dve)
            for i in range(KD):
                nc.vector.scalar_tensor_tensor(m.HN[:, i, :], m.X[:, i, :], m.p("final", i), norm.std, ALU.mult,
                                               ALU.mult).then_inc(ready, 1)

        @block.sync
        def _(sp):
            for i in range(KD):
                sp.wait_ge(ready, i + 1)
                sp.dma_start(a["out"][:, i, :], m.HN[:, i, :]).then_inc(m.stored, 16)
            sp.wait_ge(m.stored, 16 * KD)


def program(nc, a):
    with ExitStack() as ctx:
        m = Chip(nc, ctx)
        m.stream, m.cond_w = Stream(), a["cond_w"]
        stream = m.stream
        m.plans = {name: stream.place(n, kt, a["w_" + name]) for name, n, kt in STREAM if "w_" + name in a}
        stage_setup(m, a)
        stage_project(m)
        stage_mix(m)
        stage_out(m)
        stage_modulate(m, 0, 0)
        stage_m_project(m)
        stage_m_heads(m)
        stage_residual(m, "m_out", m.A[:, 8:16, :], KD, gate_of(m, 0, 0), "ffn_up")
        stage_modulate(m, 0, 1)
        stage_ffn(m)
        stage_residual(m, "ffn_down", m.A, KE, gate_of(m, 0, 1), "h_in", halves=2)
        stage_modulate(m, 1, 0)
        stage_h_project(m)
        stage_h_heads(m)
        stage_residual(m, "h_out", m.A[:, 0:8, :], KD, gate_of(m, 1, 0), None)
        stage_modulate(m, 1, 1)
        stage_route(m)
        stage_experts(m, a)
        stage_combine(m)
        stage_final(m, a)



def by_tile(np, v):
    return v.reshape(-1, P).T


def weight_blocks(np, w):
    k, n = w.shape
    return w.reshape(k // P, P, n // P, P).transpose(2, 1, 0, 3).reshape(n // P, P, k)


def lay_out(np, i):
    f = lambda v: np.ascontiguousarray(v, dtype=np.float32)
    out = {"xT": i["x"][0].T.reshape(KD, P, S).transpose(1, 0, 2),
           "memT": i["mem"][0].T.reshape(KD, P, MEM).transpose(1, 0, 2)}
    row = lambda v: np.pad(v.reshape(HEADS, 1), ((0, P - HEADS), (0, 0)))
    vectors = {"conv_a": i["conv_a_w"], "sg_g": i["sg_ln_g"], "sg_b": i["sg_ln_b"], "pool_s": i["pool_scale"],
               "dw_w": i["cc_dw_w"], "dw_b": i["cc_dw_b"], "cc_g": i["cc_ln_g"], "cc_b": i["cc_ln_b"],
               "ln_g": i["ln_g"], "ln_b": i["ln_b"], "c": i["c_2"], "ada_b": i["ada_b_2"],
               "norm1": i["norm1_w_2"], "norm2": i["norm2_w_2"], "final": i["final_norm_w_2"],
               "m_conv_w": i["m_conv_w_2"], "m_conv_b": i["m_conv_b_2"], "m_norm": i["m_norm_w_2"],
               "lb": i["h_lb_logits_2"], "h_norm": i["h_norm_w_2"]}
    out["par"] = np.concatenate([by_tile(np, vectors[n]) if n in vectors else
                                 row(i["m_i_bias_2"] if n == "mi_b" else i["m_f_bias_2"]) for n, _ in PARAMS], 1)
    s, t = np.arange(P)[:, None], np.arange(P)[None, :]
    win = np.array([[2, 4], [8, 16]])[:, :, None].repeat(64, 2).reshape(2, P).T
    consts = {"ident": s == t, "tri": s <= t, "neg": np.where(s > t, -BIG, 0.0),
              "restart": np.broadcast_to(np.arange(S) % P != 0, (P, S)),
              "pinv": (1.0 / np.minimum(np.arange(16)[None, None, :] + 1, win[:, :, None])).reshape(P, 32),
              "pwin": 1.0 / win, "eps5": np.full((P, 1), 1e-5), "eps6": np.full((P, 1), 1e-6),
              "iota": np.broadcast_to(np.arange(EXPERTS) - EXPERTS, (P, EXPERTS)), "one": np.ones((P, 1)),
              "before": s < t, "first_row": np.broadcast_to(np.arange(EXPERTS) * CAP, (P, EXPERTS)),
              "tok_id": s + P * np.arange(ST)[None, :]}
    out["cst"] = np.concatenate([consts[n].astype(np.float32) for n, _ in CONSTS], 1)
    lvl = [(s // (2 * b) == t // (2 * b)) & (s % (2 * b) < b) & (t % (2 * b) >= b) for b in (1, 2, 4, 8, 16, 32, 64)]
    out["lvl"] = np.ascontiguousarray(np.stack([s == t] + lvl, 1).astype(np.uint32))
    out["sel"] = np.repeat(np.eye(HEADS)[:, :, None], P, 2)
    out["sgw"] = i["sg_w"][0].transpose(2, 0, 1)
    out["sgb"] = i["sg_b"][0]
    out["plw"] = i["pool_w"][0]
    tiles = lambda w: w.reshape(-1, P, w.shape[1]).transpose(1, 0, 2)
    out["pw"] = tiles(i["cc_pw_w"][0])
    out["rw"] = tiles(i["moe_router_2"][0])
    m_in, up = i["m_w_in_2"][0], 2 * HEADS
    out["gw"] = tiles(m_in[:, -up:])
    order = [12, 13, 14, 15, 10, 11, 0, 1, 2, 3, 4, 5, 8, 9, 6, 7, 16, 17] + list(range(18, 28))
    out["w_in"] = weight_blocks(np, i["w_in"][0])[order]
    out["w_kv"] = weight_blocks(np, i["w_kv"][0])
    out["w_out"] = weight_blocks(np, i["w_out"][0])
    out["cond_w"] = i["ada_w_2"].reshape(2, KD, P, 6 * D // COND, COND).transpose(0, 3, 1, 2, 4).reshape(-1, P, COND)
    out["w_m_in"] = weight_blocks(np, m_in[:, :-up])
    out["w_m_out"] = weight_blocks(np, i["m_w_out_2"][0])
    out["w_h_in"] = weight_blocks(np, i["h_w_in_2"][0])
    out["w_h_out"] = weight_blocks(np, i["h_w_out_2"][0])
    pair = lambda g, u: np.stack([weight_blocks(np, g), weight_blocks(np, u)], 1).reshape(-1, P, D)
    out["w_ffn_up"] = pair(i["ffn_w_gate_2"][0], i["ffn_w_up_2"][0])
    down = i["ffn_w_down_2"][0].reshape(2, KE, P, KD, P).transpose(3, 0, 2, 1, 4)
    out["w_ffn_down"] = down.reshape(2 * KD, P, FFE)
    out["w_moe_up"] = np.stack([pair(g, u) for g, u in zip(i["moe_w_gate_2"][0], i["moe_w_up_2"][0])]).reshape(-1, P, D)
    out["w_moe_down"] = np.stack([weight_blocks(np, w) for w in i["moe_w_down_2"][0]]).reshape(-1, P, FFE)
    return {n: v if v.dtype == np.uint32 else f(v) for n, v in out.items()}


def kernel(**inputs):
    import numpy as np
    import concourse.bacc as bacc
    from concourse.bass_utils import run_bass_kernel_spmd

    arrays = lay_out(np, {n: np.asarray(v) for n, v in inputs.items()})
    nc = bacc.Bacc("TRN2", target_bir_lowering=False, num_devices=1)
    a = {n: nc.dram_tensor("in_" + n, v.shape, mybir.dt.from_np(v.dtype), kind="ExternalInput").ap()
         for n, v in arrays.items()}
    a["out"] = nc.dram_tensor("out", (P, KD, S), F32, kind="ExternalOutput").ap()
    program(nc, a)
    r = run_bass_kernel_spmd(nc, [{"in_" + n: v for n, v in arrays.items()}], core_ids=[0])
    got = r.results[0]["out"]
    return np.ascontiguousarray(got.transpose(2, 1, 0)).reshape(1, S, D)
```
